# Optimizing a Trainium2 kernel written in Bass

```python
import jax, jax.numpy as jnp
from jax import lax
import numpy as np

D_MODEL = 1024
BATCH = 1
SEQ = 512
DEPTH = 1
DEC_BATCH = 1
DEC_SEQ = 512
PAST_LEN = 128

MIX_WIDTH = D_MODEL
MLA_WIDTH = MIX_WIDTH // 2
POOL_WIDTH = MIX_WIDTH - MLA_WIDTH
N_HEADS = 8
QK_NOPE_DIM = 64
QK_ROPE_DIM = 32
QK_HEAD_DIM = QK_NOPE_DIM + QK_ROPE_DIM
V_HEAD_DIM = MLA_WIDTH // N_HEADS
Q_LORA_RANK = D_MODEL // 4
KV_LORA_RANK = D_MODEL // 8
ROPE_THETA = 10000.0
Q_BLOCK = 128
POOL_WINDOWS = (2, 4, 8, 16)
N_POOL_GROUPS = len(POOL_WINDOWS)
POOL_GROUP_DIM = POOL_WIDTH // N_POOL_GROUPS
IN_WIDTH = Q_LORA_RANK + KV_LORA_RANK + QK_ROPE_DIM + POOL_WIDTH
D_FF = 2816
CONV_WIDTH = 3
PLE_DIM = 256
EPS = 1e-6

kernel_name = 'hybrid_mla_pool_encoder'

def _rmsnorm(x, g):
    xf = x.astype(jnp.float32)
    y = xf * lax.rsqrt(jnp.mean(xf * xf, axis=-1, keepdims=True) + EPS)
    return (y * g.astype(jnp.float32)).astype(x.dtype)

def _rope_tables(seq_len, dim, dtype):
    inv = 1.0 / (ROPE_THETA ** (np.arange(0, dim, 2, dtype=np.float32) / dim))
    ang = np.arange(seq_len, dtype=np.float32)[:, None] * inv[None, :]
    emb = np.concatenate([ang, ang], axis=-1)
    return jnp.asarray(np.cos(emb), dtype), jnp.asarray(np.sin(emb), dtype)

def _rope(x, cos, sin):
    half = x.shape[-1] // 2
    rot = jnp.concatenate([-x[..., half:], x[..., :half]], axis=-1)
    return x * cos + rot * sin

def _attend(q_nope, q_rope, k_nope, k_rope, v):
    B, S, H, dn = q_nope.shape
    nb = S // Q_BLOCK
    scale = QK_HEAD_DIM ** -0.5

    def block(args):
        qn, qr = args
        s = jnp.einsum('bqhd,bkhd->bhqk', qn, k_nope) + jnp.einsum('bqhd,bkd->bhqk', qr, k_rope)
        pr = jax.nn.softmax(s.astype(jnp.float32) * scale, axis=-1).astype(v.dtype)
        return jnp.einsum('bhqk,bkhd->bqhd', pr, v)

    qn_b = q_nope.reshape(B, nb, Q_BLOCK, H, dn).transpose(1, 0, 2, 3, 4)
    qr_b = q_rope.reshape(B, nb, Q_BLOCK, H, QK_ROPE_DIM).transpose(1, 0, 2, 3, 4)
    out = lax.map(block, (qn_b, qr_b))
    return out.transpose(1, 0, 2, 3, 4).reshape(B, S, H * V_HEAD_DIM)

def _multiscale_pool(u, pool_w, pool_scale):
    B, S, C = u.shape
    uf = u.astype(jnp.float32)
    cs = jnp.concatenate([jnp.zeros((B, 1, C), jnp.float32), jnp.cumsum(uf, axis=1)], axis=1)
    t = np.arange(S)
    means = []
    for g, w in enumerate(POOL_WINDOWS):
        lo = np.clip(t - w // 2, 0, S)
        hi = np.clip(t - w // 2 + w, 0, S)
        c = cs[:, :, g * POOL_GROUP_DIM:(g + 1) * POOL_GROUP_DIM]
        cnt = jnp.asarray((hi - lo).astype(np.float32))[None, :, None]
        means.append((c[:, hi] - c[:, lo]) / cnt)
    pooled = jnp.stack(means, axis=2)
    diff = (pooled - uf.reshape(B, S, N_POOL_GROUPS, POOL_GROUP_DIM)).astype(u.dtype)
    mixed = jnp.einsum('bsgc,gcd->bsgd', diff, pool_w).reshape(B, S, C)
    return mixed * pool_scale

def _dwconv3(h, conv_w, conv_b):
    hp = jnp.pad(h, ((0, 0), (1, 1), (0, 0)))
    return hp[:, :-2] * conv_w[0] + h * conv_w[1] + hp[:, 2:] * conv_w[2] + conv_b

def _layer(x, p, norm1, w_in, q_a_norm, w_q_b, kv_a_norm, w_kv_b, pool_w, pool_scale, w_out,
           norm2, w_up, conv_w, conv_b, w_down, norm3, w_ple_gate, b_ple_gate, w_ple_proj):
    B, S, _ = x.shape
    h = _rmsnorm(x, norm1) @ w_in
    o1 = Q_LORA_RANK
    o2 = o1 + KV_LORA_RANK
    o3 = o2 + QK_ROPE_DIM
    c_q, c_kv, k_rope, u = h[..., :o1], h[..., o1:o2], h[..., o2:o3], h[..., o3:]
    q = jnp.einsum('bsr,rhd->bshd', _rmsnorm(c_q, q_a_norm), w_q_b)
    kv = jnp.einsum('bsr,rhd->bshd', _rmsnorm(c_kv, kv_a_norm), w_kv_b)
    q_nope, q_rope = q[..., :QK_NOPE_DIM], q[..., QK_NOPE_DIM:]
    k_nope, v = kv[..., :QK_NOPE_DIM], kv[..., QK_NOPE_DIM:]
    cos, sin = _rope_tables(S, QK_ROPE_DIM, x.dtype)
    q_rope = _rope(q_rope, cos[:, None, :], sin[:, None, :])
    k_rope = _rope(k_rope, cos, sin)
    attn = _attend(q_nope, q_rope, k_nope, k_rope, v)
    pool = _multiscale_pool(u, pool_w, pool_scale)
    x = x + jnp.concatenate([attn, pool], axis=-1) @ w_out
    up = _dwconv3(_rmsnorm(x, norm2) @ w_up, conv_w, conv_b)
    gate, val = up[..., :D_FF], up[..., D_FF:]
    x = x + (jax.nn.silu(gate) * val) @ w_down
    g = jax.nn.sigmoid(_rmsnorm(x, norm3) @ w_ple_gate + b_ple_gate)
    x = x + (p @ w_ple_proj) * g
    return x

def _trunk(x, p, norm1, w_in, q_a_norm, w_q_b, kv_a_norm, w_kv_b, pool_w, pool_scale, w_out,
           norm2, w_up, conv_w, conv_b, w_down, norm3, w_ple_gate, b_ple_gate, w_ple_proj, final_norm):
    for i in range(DEPTH):
        x = _layer(x, p[i], norm1[i], w_in[i], q_a_norm[i], w_q_b[i], kv_a_norm[i], w_kv_b[i],
                   pool_w[i], pool_scale[i], w_out[i], norm2[i], w_up[i], conv_w[i], conv_b[i],
                   w_down[i], norm3[i], w_ple_gate[i], b_ple_gate[i], w_ple_proj[i])
    return _rmsnorm(x, final_norm)

def setup_inputs(seed: int = 0) -> dict:
    key = jax.random.key(seed)
    ks = jax.random.split(key, 24)
    f32 = jnp.float32

    def nrm(k, shape, fan_in):
        return jax.random.normal(k, shape, f32) * (fan_in ** -0.5)

    def gain(k, shape):
        return 1.0 + 0.05 * jax.random.normal(k, shape, f32)

    L = DEPTH
    return {
        'x_prompt': jax.random.normal(ks[0], (BATCH, SEQ, D_MODEL), f32),
        'x_sample': jax.random.normal(ks[1], (DEC_BATCH, DEC_SEQ, D_MODEL), f32),
        'p_prompt': jax.random.normal(ks[2], (DEPTH, BATCH, SEQ, PLE_DIM), f32),
        'p_sample': jax.random.normal(ks[3], (DEPTH, DEC_BATCH, DEC_SEQ, PLE_DIM), f32),
        'norm1': gain(ks[4], (L, D_MODEL)),
        'w_in': nrm(ks[5], (L, D_MODEL, IN_WIDTH), D_MODEL),
        'q_a_norm': gain(ks[6], (L, Q_LORA_RANK)),
        'w_q_b': nrm(ks[7], (L, Q_LORA_RANK, N_HEADS, QK_HEAD_DIM), Q_LORA_RANK),
        'kv_a_norm': gain(ks[8], (L, KV_LORA_RANK)),
        'w_kv_b': nrm(ks[9], (L, KV_LORA_RANK, N_HEADS, QK_NOPE_DIM + V_HEAD_DIM), KV_LORA_RANK),
        'pool_w': nrm(ks[10], (L, N_POOL_GROUPS, POOL_GROUP_DIM, POOL_GROUP_DIM), POOL_GROUP_DIM),
        'pool_scale': gain(ks[11], (L, POOL_WIDTH)),
        'w_out': nrm(ks[12], (L, MIX_WIDTH, D_MODEL), MIX_WIDTH),
        'norm2': gain(ks[13], (L, D_MODEL)),
        'w_up': nrm(ks[14], (L, D_MODEL, 2 * D_FF), D_MODEL),
        'conv_w': nrm(ks[15], (L, CONV_WIDTH, 2 * D_FF), CONV_WIDTH),
        'conv_b': 0.02 * jax.random.normal(ks[16], (L, 2 * D_FF), f32),
        'w_down': nrm(ks[17], (L, D_FF, D_MODEL), D_FF),
        'norm3': gain(ks[18], (L, D_MODEL)),
        'w_ple_gate': nrm(ks[19], (L, D_MODEL, D_MODEL), D_MODEL),
        'b_ple_gate': 0.02 * jax.random.normal(ks[20], (L, D_MODEL), f32),
        'w_ple_proj': nrm(ks[21], (L, PLE_DIM, D_MODEL), PLE_DIM),
        'final_norm': gain(ks[22], (D_MODEL,)),
    }

def reference(x_prompt, x_sample, p_prompt, p_sample, norm1, w_in, q_a_norm, w_q_b, kv_a_norm, w_kv_b,
              pool_w, pool_scale, w_out, norm2, w_up, conv_w, conv_b, w_down, norm3, w_ple_gate,
              b_ple_gate, w_ple_proj, final_norm):
    y_prompt = _trunk(x_prompt, p_prompt, norm1, w_in, q_a_norm, w_q_b, kv_a_norm, w_kv_b, pool_w,
                      pool_scale, w_out, norm2, w_up, conv_w, conv_b, w_down, norm3, w_ple_gate,
                      b_ple_gate, w_ple_proj, final_norm)
    y_sample = _trunk(x_sample, p_sample, norm1, w_in, q_a_norm, w_q_b, kv_a_norm, w_kv_b, pool_w,
                      pool_scale, w_out, norm2, w_up, conv_w, conv_b, w_down, norm3, w_ple_gate,
                      b_ple_gate, w_ple_proj, final_norm)
    return (y_prompt, y_sample)


_drawn_inputs = setup_inputs


def setup_inputs(seed=0):
    import zlib

    import numpy as np

    out = dict(_drawn_inputs(seed))
    spreads = {}
    factors = {'q_a_norm': 8.0,
     'kv_a_norm': 8.0,
     'conv_b': 18.047,
     'norm3': 200.0,
     'b_ple_gate': 200.0,
     'pool_scale': 8.0,
     'norm2': 6.879,
     'p_prompt': 2.794,
     'p_sample': 2.796,
     'w_ple_gate': 3.976,
     'w_ple_proj': 2.785}
    for name, (base, spread) in spreads.items():
        noise = np.random.default_rng([zlib.crc32(name.encode()), seed]).standard_normal(out[name].shape)
        drawn = base * np.exp(spread * noise) if base else spread * noise
        out[name] = __import__('jax').numpy.asarray(drawn.astype(out[name].dtype))
    for name, factor in factors.items():
        out[name] = (out[name] * factor).astype(out[name].dtype)
    return out
```

```python
from contextlib import ExitStack

import numpy as np

import concourse.bass as bass
from concourse import mybir

F32 = mybir.dt.float32
F32R = mybir.dt.float32r
ACT = mybir.ActivationFunctionType
ALU = mybir.AluOpType
AX_X = mybir.AxisListType.X

P = 128
D = 1024
S = 512
NSEQ = 2
KT = D // P
TT = S // P
Q_RANK, KV_RANK, ROPE, NOPE, V_DIM, HEADS = 256, 128, 32, 64, 64, 8
HEAD = NOPE + ROPE
POOL_WINDOWS = (2, 4, 8, 16)
PAD = 8
UB = S + 2 * PAD
FF = 2816
FT = FF // P
NPAIR = FT // 2
EPS = 1e-6

N1 = 4 * 2 * FT
N2, N3, GQ = N1 + KT, N1 + 2 * KT, N1 + 3 * KT
GKV, PSC, BG = GQ + 2, GQ + 3, GQ + 7
NPAR = BG + KT

T_IN, T_POOL, T_ATT, T_OUT = 0, 8, 9, 17
T_UP = T_OUT + NSEQ * KT
T_GATE = T_UP + 4 * NPAIR

B_X, B_KV, B_Q, B_X2, B_X3 = 0, 2, 4, 6, 8


def encoder(nc, x, p_in, w, y, consts):
    with ExitStack() as ctx:
        def sb(name, shape, dt=F32):
            return ctx.enter_context(nc.sbuf_tensor(name, shape, dt))

        def sem(name):
            return ctx.enter_context(nc.semaphore(name))

        XT = sb("XT", [P, NSEQ * KT * S])
        XH = sb("XH", [P, NSEQ, KT, S], F32R)
        XL = sb("XL", [P, NSEQ, KT, S], F32R)
        xt = XT[:, :].rearrange("p (s k t) -> p s k t", s=NSEQ, k=KT)
        R = sb("R", [P, NSEQ, S])
        ident = sb("ident", [P, P])
        ones = sb("ones", [P, P])
        par = sb("par", [P, NPAR])
        WR = sb("WR", [P, 2, KT, P])
        WH = sb("WH", [P, 2, KT, P], F32R)
        WL = sb("WL", [P, 2, KT, P], F32R)
        diag = sb("diag", [P, TT, P])
        edge = sb("edge", [P, 4, 2 * PAD])
        V_COL, R_COL, SSX, NB, RS, RC, FS, FV, FR, HALF, CP = 0, 40, 80, 88, 92, 96, 100, 116, 124, 132, 140
        col = sb("col", [P, CP + 16])
        SF = sb("SF", [P, 5124])
        with ExitStack() as tail:
            TL = tail.enter_context(nc.sbuf_tensor("TL", [P, 3 * D], F32))
        GHL = sb("GHL", [P, 2, 2, NSEQ, S], F32R)
        WDHL = sb("WDHL", [P, 2, 2, D], F32R)
        CHL = sb("CHL", [P, 2, 3, NSEQ, S], F32R)

        xtok = SF[:, 0:4096].rearrange("p (a d) -> p a d", a=4)
        prow = XT[:, 8192 - 512:8192 - 128].rearrange("p (a d) -> p a d", a=3)
        SQ = SF[:, 0:1024].rearrange("p (s t) -> p s t", s=NSEQ)
        SQT = SF[:, 1028:1540]
        ub = SF[:, 1540:1540 + 2 * UB].rearrange("p (s t) -> p s t", s=NSEQ)
        w1, w2 = SF[:, 2596:2596 + UB], SF[:, 3124:3124 + UB]
        tab_q, tab_k = SF[:, 4096:4608], SF[:, 4608:5120]
        PD = XT[:, 0:4096].rearrange("p (s g t) -> p s g t", s=NSEQ, g=4)
        cs = XT[:, 4096:7168].rearrange("p (c s t) -> p c s t", c=3, s=NSEQ)
        PT = XT[:, 0:4096].rearrange("p (a k q) -> p a k q", a=2, k=TT)
        PB = XT[:, 4096:5632].rearrange("p (a k) -> p a k", a=3)
        VB = XT[:, 5632:6656].rearrange("p (k d) -> p k d", d=P)
        QF = XT[:, 6656:7680].rearrange("p (a t) -> p a t", a=2)
        QTMP = XT[:, 7680:8192]
        QH, QL = GHL[:, 0], GHL[:, 1]
        KH = WDHL[:, 0].rearrange("p h (s t) -> p h s t", s=NSEQ)
        KL = WDHL[:, 1].rearrange("p h (s t) -> p h s t", s=NSEQ)
        U = SF[:, 0:1028].rearrange("p (s t) -> p s t", s=NSEQ)
        C = SF[:, 1028:2052].rearrange("p (s t) -> p s t", s=NSEQ)
        SG = SF[:, 2052:3076].rearrange("p (s t) -> p s t", s=NSEQ)
        WDR = SF[:, 3076:5124].rearrange("p (k m) -> p k m", k=2)
        ptok = SF[:, 2052:3076].rearrange("p (t d) -> p t d", t=TT)
        PLR = SF[:, 3076:3588].rearrange("p (a k m) -> p a k m", a=2, k=2)
        GZ = SF[:, 3588:4612].rearrange("p (a t) -> p a t", a=2)
        GS = [SF[:, 4612:5124], SF[:, 1540:2052]]
        PLH = WDHL[:, 0].rearrange("p k (a m) -> p a k m", m=P)
        PLL = WDHL[:, 1].rearrange("p k (a m) -> p a k m", m=P)
        PH, PL = CHL[:, 0], CHL[:, 1]
        gain_row = TL[:, 0:D]
        OT = TL[:, D:3 * D].rearrange("p (a d) -> p a d", a=2)

        ps = [ctx.enter_context(nc.psum_tensor(f"ps{b}", [P, 512], F32)) for b in range(8)]
        xt_dram = nc.dram_tensor("xt_scratch", (P, NSEQ * KT * S), F32, kind="Internal").ap()

        ident_in, gains_in, taps_in, tabs_in, edge_in, row_in = (sem(n) for n in (
            "ident_in", "gains_in", "taps_in", "tabs_in", "edge_in", "row_in"))
        x_in = [sem(f"x_in{i}") for i in range(4)]
        win_in = [sem(f"win_in{i}") for i in range(2)]
        ring_in = [sem(f"ring_in{i}") for i in range(2)]
        poolw_in, wq_in, wkv_in = sem("poolw_in"), sem("wq_in"), sem("wkv_in")
        ple_in = [sem(f"ple_in{i}") for i in range(2)]
        wd_in, p_in_sem = sem("wd_in"), sem("p_tokens_in")
        xt_spilled = sem("xt_spilled")
        xt_back = [sem(f"xt_back{i}") for i in range(4)]
        out_done = [sem(f"out_done{i}") for i in range(2)]
        w_hi, w_lo, rot_done = sem("w_hi"), sem("w_lo"), sem("rot_done")
        consts_set, par_tr, par_copied = sem("consts_set"), sem("par_tr"), sem("par_copied")
        x_tr, x_hi, x_split, x_sq = sem("x_tr"), sem("x_hi"), sem("x_split"), sem("x_sq")
        v_ready, col_ready, diag_ready, rb_ready = sem("v_ready"), sem("col_ready"), sem("diag_ready"), sem("rb_ready")
        r_copied, sq_ready, ss_ready = sem("r_copied"), sem("sq_ready"), sem("ss_ready")
        acc_ready, acc_free = sem("acc_ready"), sem("acc_free")
        kr_step, kr_ready, kr_hi, kr_done = sem("kr_step"), sem("kr_ready"), sem("kr_hi"), sem("kr_done")
        cs_ready, c_applied, c_hi, c_lo = sem("cs_ready"), sem("c_applied"), sem("c_hi"), sem("c_lo")
        sq_part, pads_zero, chain, diff_ready = sem("sq_part"), sem("pads_zero"), sem("chain"), sem("diff_ready")
        d_hi, d_lo, mix_ready, mix_hi, mix_lo = sem("d_hi"), sem("d_lo"), sem("mix_ready"), sem("mix_hi"), sem("mix_lo")
        q_proj, k_proj, v_proj, v_copied = sem("q_proj"), sem("k_proj"), sem("v_proj"), sem("v_copied")
        q_step, q_rot, qf_ready, q_hi, q_lo = sem("q_step"), sem("q_rot"), sem("qf_ready"), sem("q_hi"), sem("q_lo")
        k_hi, k_lo = sem("k_hi"), sem("k_lo")
        s_ready, max_ready, exp_done, rc_ready, p_norm = (sem(n) for n in (
            "s_ready", "max_ready", "exp_done", "rc_ready", "p_norm"))
        p_tr, pt_ready, o_ready, o_hi, o_lo = (sem(n) for n in ("p_tr", "pt_ready", "o_ready", "o_hi", "o_lo"))
        wo_ready, x2_ready, sq_mul, sq_sum = sem("wo_ready"), sem("x2_ready"), sem("sq_mul"), sem("sq_sum")
        sq_zero = sem("sq_zero")
        x2_hi, x2_lo = sem("x2_hi"), sem("x2_lo")
        up_ready, u_ready, tap1, tap0, conv_done, silu_done, g_ready = (sem(n) for n in (
            "up_ready", "u_ready", "tap1", "tap0", "conv_done", "silu_done", "g_ready"))
        cp_ready, u_pads = sem("cp_ready"), sem("u_pads")
        g_hi, g_lo, wd_hi, wd_lo, dn_ready, dn_free = (sem(n) for n in (
            "g_hi", "g_lo", "wd_hi", "wd_lo", "dn_ready", "dn_free"))
        x3_hi, x3_lo, p_tr_ready, p_hi, p_lo = (sem(n) for n in ("x3_hi", "x3_lo", "p_tr_ready", "p_hi", "p_lo"))
        pl_hi, pl_lo, pl_used = sem("pl_hi"), sem("pl_lo"), sem("pl_used")
        gate_ready, ple_ready, gz_ready, sig_ready, gp_ready, x4_ready = (sem(n) for n in (
            "gate_ready", "ple_ready", "gz_ready", "sig_ready", "gp_ready", "x4_ready"))
        f_tr, f_sq, f_sum, f_v, f_r, f_out = (sem(n) for n in ("f_tr", "f_sq", "f_sum", "f_v", "f_r", "f_out"))

        block = ctx.enter_context(nc.Block())

        def slot(n):
            return n % 2

        def mm3(pe, out, wh, wl, xh, xl, first, last):
            pe.matmul(out, wh, xh, start=first, stop=False)
            pe.matmul(out, wh, xl, start=False, stop=False)
            return pe.matmul(out, wl, xh, start=False, stop=last)

        def split_w_hi(act, n, free, count, cols=KT):
            if free is not None:
                act.wait_ge(free, count)
            act.activation(WH[:, slot(n), 0:cols, :], WR[:, slot(n), 0:cols, :], ACT.Copy).then_inc(w_hi, 1)

        def split_w_lo(dve, n, count, cols=KT):
            dve.wait_ge(w_hi, count + 1)
            dve.tensor_tensor(WL[:, slot(n), 0:cols, :], WR[:, slot(n), 0:cols, :],
                              WH[:, slot(n), 0:cols, :].bitcast(F32), ALU.subtract).then_inc(w_lo, 1)

        def wtile(v):
            return v.rearrange("(k p) m -> p k m", p=P)

        @block.sync
        def _(sp):
            sp.dma_start(ident[:, :], consts["ident"]).then_inc(ident_in, 16)
            for t in range(TT):
                sp.dma_start(xtok[:, t, :], x[0][t * P:(t + 1) * P, :]).then_inc(x_in[t], 16)
            cols_in = [320, 256, 0, 128] + [416 + g * P for g in range(4)]
            for n in range(2):
                sp.dma_start(WR[:, n, :, :], wtile(w["w_in"][:, cols_in[n]:cols_in[n] + P])).then_inc(win_in[n], 16)
            for t in range(TT):
                if t == 0:
                    sp.wait_ge(x_tr, KT)
                sp.wait_ge(x_sq, t + 1)
                sp.dma_start(xtok[:, t, :], x[1][t * P:(t + 1) * P, :]).then_inc(x_in[t], 16)
            sp.wait_ge(x_sq, 2 * TT)
            sp.dma_start(tab_q, consts["rope_q"]).then_inc(tabs_in, 16)
            sp.dma_start(tab_k, consts["rope_k"]).then_inc(tabs_in, 16)
            sp.dma_start(edge[:, :, :], consts["pool_edge"].partition_broadcast(P)).then_inc(edge_in, 16)
            sp.wait_ge(x_split, 2 * KT)
            sp.dma_start(xt_dram, XT[:, :]).then_inc(xt_spilled, 16)
            for n in range(2, 8):
                sp.wait_ge(w_lo, n - 1)
                sp.dma_start(WR[:, slot(n), :, :], wtile(w["w_in"][:, cols_in[n]:cols_in[n] + P])).then_inc(win_in[slot(n)], 16)
            sp.wait_ge(w_lo, T_POOL - 1)
            sp.dma_start(WR[:, slot(T_POOL), 0:4, :], w["pool_w"].rearrange("g c d -> c g d")).then_inc(poolw_in, 16)
            with sp.Fori(0, HEADS // 2) as i:
                sp.wait_ge(w_lo, i * 2 + (T_ATT - 1))
                for k in range(2):
                    sp.dma_start(WR[:, slot(T_ATT), 2 * k:2 * k + 2, 0:HEAD],
                                 w["w_q_b"][k * P:(k + 1) * P, bass.ds(i * 2, 2), :]).then_inc(wq_in, 16)
                sp.wait_ge(w_lo, i * 2 + T_ATT)
                sp.dma_start(WR[:, slot(T_ATT + 1), 0:2, :], w["w_kv_b"][:, bass.ds(i * 2, 2), :]).then_inc(wkv_in, 16)
            for s in range(NSEQ):
                if s == 0:
                    for n in range(T_OUT, T_OUT + 2):
                        sp.wait_ge(w_lo, n - 1)
                        sp.dma_start(WR[:, slot(n), :, :], wtile(w["w_out"][:, (n - T_OUT) * P:(n - T_OUT + 1) * P])).then_inc(ring_in[slot(n)], 16)
                    sp.wait_ge(o_lo, 2 * HEADS)
                    for q in range(4):
                        sp.dma_start(XT[:, q * 2048:(q + 1) * 2048], xt_dram[:, q * 2048:(q + 1) * 2048]).then_inc(xt_back[q], 16)
                with sp.Fori(1 - s, KT // 2) as i:
                    for c in range(2):
                        n = T_OUT + s * KT + c
                        sp.wait_ge(w_lo, i * 2 + (n - 1))
                        sp.dma_start(WR[:, slot(n), :, :], wtile(w["w_out"][:, bass.ds(i * P * 2 + c * P, P)])).then_inc(ring_in[slot(n)], 16)
            def load_pair(i, first=False):
                for c in range(4):
                    n = T_UP + c
                    f = (c // 2) * P + (c % 2) * FF
                    sp.wait_ge(w_lo, i * 4 + (n - 1))
                    sp.dma_start(WR[:, slot(n), :, :], wtile(w["w_up"][:, bass.ds(i * 2 * P + f, P)])).then_inc(ring_in[slot(n)], 16)
                    if c == 1:
                        if not first:
                            sp.wait_ge(wd_lo, i)
                        sp.dma_start(WDR, w["w_down"][bass.ds(i * 2 * P, 2 * P), :].rearrange("(k p) m -> p k m", p=P)).then_inc(wd_in, 16)

            load_pair(0, first=True)
            with sp.Fori(1, NPAIR) as i:
                load_pair(i)

            def store(s):
                for t in range(TT):
                    sp.wait_ge(f_out, 2 * (s * TT + t + 1))
                    sp.dma_start(y[s][t * P:(t + 1) * P, :], OT[:, t % 2, :]).then_inc(out_done[t % 2], 16)

            for s in range(NSEQ):
                def gate_load(i, c):
                    n = T_GATE + s * KT + c
                    sp.wait_ge(w_lo, i * 2 + (n - 1))
                    sp.dma_start(WR[:, slot(n), :, :], wtile(w["w_ple_gate"][:, bass.ds(i * P * 2 + c * P, P)])).then_inc(ring_in[slot(n)], 16)

                def ple_load(i, c):
                    sp.dma_start(PLR[:, c], wtile(w["w_ple_proj"][:, bass.ds(i * P * 2 + c * P, P)])).then_inc(ple_in[c], 16)

                if s == 0:
                    gate_load(0, 0)
                    gate_load(0, 1)
                    sp.wait_ge(wd_lo, NPAIR)
                    ple_load(0, 0)
                    ple_load(0, 1)
                    sp.wait_ge(g_lo, 4 * NPAIR)
                else:
                    sp.wait_ge(p_tr_ready, 2)
                sp.dma_start(ptok, p_in[s].rearrange("(t p) d -> p t d", p=P)).then_inc(p_in_sem, 16)
                def both_loads(i):
                    for c in range(2):
                        gate_load(i, c)
                        sp.wait_ge(pl_lo, i * 2 + (s * KT + c - 1))
                        ple_load(i, c)

                with sp.Fori(1 - s, KT // 2 - s) as i:
                    both_loads(i)
                if s == 0:
                    sp.wait_ge(dn_ready, 16 * NPAIR)
                    sp.dma_start(gain_row, w["final_norm"].partition_broadcast(P)).then_inc(row_in, 16)
                else:
                    store(0)
                    both_loads(KT // 2 - 1)
            store(1)
            for a in range(2):
                sp.wait_ge(out_done[a], 16 * NSEQ * TT // 2)

        @block.tensor
        def _(pe):
            def x_unit(u):
                s, f = divmod(u, KT)
                if f == 0:
                    for t in range(TT):
                        pe.wait_ge(x_in[t], 16 * (s + 1))
                if u >= 3:
                    pe.wait_ge(x_split, u - 2)
                b = ps[4 + u % 3]
                for t in range(TT):
                    ins = pe.transpose(b[:, t * P:(t + 1) * P], xtok[:, t, f * P:(f + 1) * P], ident[:, :])
                ins.then_inc(x_tr, 1)

            def in_tile(n, s, kts=range(KT), fresh=False):
                for k in kts:
                    if fresh:
                        pe.wait_ge(x_split, s * KT + k + 1)
                    ins = mm3(pe, ps[2 * (n % 2) + s][:, :], WH[:, slot(n), k, :], WL[:, slot(n), k, :],
                              XH[:, s, k, :], XL[:, s, k, :], k == 0, k == KT - 1)
                    if k == KT - 1:
                        ins.then_inc(acc_ready, 1)

            def sums(bank, s):
                for t in range(TT):
                    ins = pe.matmul(ps[bank][:, s * TT + t:s * TT + t + 1], SQ[:, s, t * P:(t + 1) * P], ones[:, 0:1],
                                    start=True, stop=True)
                return ins

            def spread(q, bank):
                pe.wait_ge(diag_ready, q + 1)
                pe.matmul(ps[bank][:, :], ones[:, :], diag[:, :, :], start=True, stop=True).then_inc(rb_ready, 1)

            pe.wait_ge(ident_in, 16)
            pe.wait_ge(gains_in, 16 * 7)
            pe.transpose(ps[7][:, 0:NPAR - N1], prow[0:NPAR - N1, 2, :], ident[0:NPAR - N1, 0:NPAR - N1]).then_inc(par_tr, 1)
            for u in range(KT):
                x_unit(u)
            pe.wait_ge(taps_in, 16 * 4)
            pe.wait_ge(par_copied, 1)
            pe.transpose(ps[7][:, 0:88], prow[0:88, 0, :], ident[0:88, 0:88])
            pe.transpose(ps[7][:, 88:176], prow[0:88, 1, :], ident[0:88, 0:88]).then_inc(par_tr, 1)
            pe.wait_ge(w_lo, 1)
            for k in range(KT):
                in_tile(0, 0, [k], fresh=True)
                x_unit(KT + k)
            in_tile(0, 1, fresh=True)
            spread(B_X, 4)
            spread(B_X + 1, 5)
            for n in range(1, 8):
                pe.wait_ge(w_lo, n + 1)
                for s in range(NSEQ):
                    if n >= 2:
                        pe.wait_ge(acc_free, 2 * (n - 2) + s + 1)
                    in_tile(n, s)
                if n == 2:
                    pe.wait_ge(sq_ready, 2)
                    for s in range(NSEQ):
                        ins = sums(6, s)
                    ins.then_inc(ss_ready, 1)
                if n == 3:
                    pe.wait_ge(r_copied, 2)
                    spread(B_KV, 4)
                    spread(B_KV + 1, 5)
                if n == 4:
                    pe.wait_ge(sq_ready, 4)
                    for s in range(NSEQ):
                        ins = sums(6, s)
                    ins.then_inc(ss_ready, 1)
                if n == 5:
                    pe.wait_ge(c_applied, 2)
                    spread(B_Q, 4)
                    spread(B_Q + 1, 5)
            pe.wait_ge(w_lo, T_POOL + 1)
            for g in range(4):
                for s in range(NSEQ):
                    q = g * 2 + s
                    pe.wait_ge(d_lo, q + 1)
                    if q >= 2:
                        pe.wait_ge(mix_lo, q - 1)
                    if q == 0:
                        pe.wait_ge(v_ready, 3)
                    ins = mm3(pe, ps[6 + q % 2][:, :], WH[:, slot(T_POOL), g, :], WL[:, slot(T_POOL), g, :],
                              XH[:, s, 4 + g, :], XL[:, s, 4 + g, :], True, True)
                    ins.then_inc(mix_ready, 1)

            pe.wait_ge(c_lo, 6)
            pe.wait_ge(kr_done, 4)
            pe.wait_ge(acc_free, 16)
            pe.wait_ge(mix_lo, 8)

            def project(i, j):
                h, s = divmod(j, 2)
                if j == 0:
                    pe.wait_ge(w_lo, i * 2 + (T_ATT + 2))
                if not isinstance(i, int) or i or j:
                    pe.wait_ge(qf_ready, i * 4 + j)
                    pe.wait_ge(k_lo, i * 4 + j)
                for k in range(2):
                    ins = mm3(pe, ps[0][:, :], WH[:, slot(T_ATT), 2 * k + h, :], WL[:, slot(T_ATT), 2 * k + h, :],
                              CHL[:, 0, k, s, :], CHL[:, 1, k, s, :], k == 0, k == 1)
                ins.then_inc(q_proj, 1)
                ins = mm3(pe, ps[1][:, :], WH[:, slot(T_ATT + 1), h, :], WL[:, slot(T_ATT + 1), h, :],
                          CHL[:, 0, 2, s, :], CHL[:, 1, 2, s, :], True, True)
                ins.then_inc(k_proj, 1)

            def values(i, s):
                if not isinstance(i, int) or i:
                    pe.wait_ge(o_lo, i * 4 + s - 1)
                for t in range(TT):
                    tok = slice(t * P, (t + 1) * P)
                    o = ps[6 + s][:, t * P:(t + 1) * P]
                    vh = WH[:, slot(T_ATT + 1), 0:2, NOPE:P]
                    vl = WL[:, slot(T_ATT + 1), 0:2, NOPE:P]
                    pe.matmul(o, CHL[:, 0, 2, s, tok], vh, start=True, stop=False)
                    pe.matmul(o, CHL[:, 0, 2, s, tok], vl, start=False, stop=False)
                    ins = pe.matmul(o, CHL[:, 1, 2, s, tok], vh, start=False, stop=True)
                ins.then_inc(v_proj, 1)

            def pair(i, last):
                def scores(u):
                    j, t = divmod(u, TT)
                    h, s = divmod(j, 2)
                    if t == 0:
                        pe.wait_ge(q_lo, i * 4 + j + 1)
                        pe.wait_ge(k_lo, i * 4 + j + 1)
                    if u >= 2:
                        pe.wait_ge(exp_done, i * 16 + u - 1)
                    tok = slice(t * P, (t + 1) * P)
                    ins = mm3(pe, ps[2 + u % 2][:, :], QH[0:HEAD, h, s, tok], QL[0:HEAD, h, s, tok],
                              KH[0:HEAD, h, s, :], KL[0:HEAD, h, s, :], True, True)
                    ins.then_inc(s_ready, 1)

                def turn(u):
                    pe.wait_ge(p_norm, i * 16 + u + 1)
                    if u >= 2:
                        pe.wait_ge(pt_ready, i * 16 + u - 1)
                    for k in range(TT):
                        ins = pe.transpose(ps[4 + u % 2][:, k * P:(k + 1) * P], PB[:, u % 3, k * P:(k + 1) * P], ident[:, :])
                    ins.then_inc(p_tr, 1)

                def weigh(j):
                    h, s = divmod(j, 2)
                    pe.wait_ge(pt_ready, i * 16 + TT * (j + 1))
                    if j < 2:
                        pe.wait_ge(v_copied, i * 2 + 2)
                    else:
                        pe.wait_ge(o_lo, i * 4 + j - 1)
                    for k in range(TT):
                        ins = pe.matmul(ps[6 + j % 2][h * V_DIM:(h + 1) * V_DIM, :], VB[:, s * TT + k, h * V_DIM:(h + 1) * V_DIM],
                                        PT[:, j % 2, k, :], start=(k == 0), stop=(k == TT - 1))
                    ins.then_inc(o_ready, 1)

                for u in range(4 * TT + 3):
                    if u < 4 * TT:
                        scores(u)
                    if u % TT == 0 and u // TT < 3:
                        project(i, u // TT + 1)
                    if u == 4 * TT and not last:
                        project(i + 1, 0)
                    if 2 <= u < 4 * TT + 2:
                        turn(u - 2)
                    if u >= TT + 2 and (u - TT - 2) % TT == 0:
                        weigh((u - TT - 2) // TT)

                if not last:
                    values(i + 1, 0)
                    values(i + 1, 1)

            project(0, 0)
            values(0, 0)
            values(0, 1)
            with pe.Fori(0, HEADS // 2 - 1) as i:
                pair(i, False)
            pair(HEADS // 2 - 1, True)

            pe.wait_ge(o_lo, 2 * HEADS)
            def out_tile(s, i, c, fresh=False):
                n = T_OUT + s * KT + c
                pe.wait_ge(w_lo, i * 4 + (n + 1))
                if not fresh:
                    pe.wait_ge(x2_ready, i * 4 + (s * KT + c - 3))
                for k in range(KT):
                    ins = mm3(pe, ps[c][:, :], WH[:, slot(n), k, :], WL[:, slot(n), k, :],
                              XH[:, s, k, :], XL[:, s, k, :], k == 0, k == KT - 1)
                ins.then_inc(wo_ready, 1)

            for m in range(KT):
                out_tile(0, m // 4, m % 4, fresh=m < 4)
            with pe.Fori(0, KT // 4) as i:
                for c in range(4):
                    out_tile(1, i, c)

            def up(i, c, fresh=False):
                n = T_UP + c
                pe.wait_ge(w_lo, i * 4 + (n + 1))
                for s in range(NSEQ):
                    if c >= 2:
                        pe.wait_ge(u_ready, i * 8 + 2 * (c - 2) + s + 1)
                    elif not fresh:
                        pe.wait_ge(u_ready, i * 8 + (2 * c + s - 3))
                    for k in range(KT):
                        if fresh and c == 0:
                            pe.wait_ge(x2_lo, s * KT + k + 1)
                        ins = mm3(pe, ps[2 * (c % 2) + s][:, :], WH[:, slot(n), k, :], WL[:, slot(n), k, :],
                                  XH[:, s, k, :], XL[:, s, k, :], k == 0, k == KT - 1)
                    ins.then_inc(up_ready, 1)

            def down(i, s):
                if s == 0:
                    pe.wait_ge(wd_lo, i + 1)
                    pe.wait_ge(g_lo, i * 4 + 4)
                for m in range(KT):
                    g = s * KT + m
                    if g >= 4:
                        pe.wait_ge(dn_free, i * 16 + g - 3)
                    for k in range(2):
                        ms = slice(m * P, (m + 1) * P)
                        ins = mm3(pe, ps[4 + g % 4][:, :], WDHL[:, 0, k, ms], WDHL[:, 1, k, ms],
                                  GHL[:, 0, k, s, :], GHL[:, 1, k, s, :], k == 0, k == 1)
                    ins.then_inc(dn_ready, 1)

            up(0, 0, fresh=True)
            pe.wait_ge(sq_sum, 16)
            for s in range(NSEQ):
                ins = sums(6, s)
            ins.then_inc(ss_ready, 1)
            up(0, 1, fresh=True)
            spread(B_X2, 4)
            spread(B_X2 + 1, 5)
            up(0, 2)
            up(0, 3)
            with pe.Fori(1, NPAIR) as i:
                up(i, 0)
                up(i, 1)
                down(i - 1, 0)
                down(i - 1, 1)
                up(i, 2)
                up(i, 3)

            def turn_p(s):
                pe.wait_ge(p_in_sem, 16 * (s + 1))
                for k in range(2):
                    if s == 1:
                        pe.wait_ge(p_lo, k + 1)
                    for t in range(TT):
                        ins = pe.transpose(ps[2 + k][:, t * P:(t + 1) * P], ptok[:, t, k * P:(k + 1) * P], ident[:, :])
                    ins.then_inc(p_tr_ready, 1)

            down(NPAIR - 1, 0)
            pe.wait_ge(u_ready, 8 * NPAIR)
            turn_p(0)
            down(NPAIR - 1, 1)

            def gate(s, i, c):
                n = T_GATE + s * KT + c
                pe.wait_ge(w_lo, i * 2 + (n + 1))
                if not isinstance(i, int) or i > 0 or s:
                    pe.wait_ge(gz_ready, i * 2 + (s * KT + c - 1))
                for k in range(KT):
                    if s == 0 and isinstance(i, int) and i == 0 and c == 0:
                        pe.wait_ge(x3_lo, k + 1)
                    ins = mm3(pe, ps[c][:, :], WH[:, slot(n), k, :], WL[:, slot(n), k, :],
                              XH[:, s, k, :], XL[:, s, k, :], k == 0, k == KT - 1)
                ins.then_inc(gate_ready, 1)
                pe.wait_ge(pl_lo, i * 2 + (s * KT + c + 1))
                if not isinstance(i, int) or i > 0 or s:
                    pe.wait_ge(gp_ready, i * 2 + (s * KT + c - 1))
                for k in range(2):
                    ins = mm3(pe, ps[4 + c][:, :], PLH[:, c, k, :], PLL[:, c, k, :],
                              PH[:, k, s, :], PL[:, k, s, :], k == 0, k == 1)
                ins.then_inc(ple_ready, 1)

            def turn_x4(s):
                for t in range(TT):
                    for h in range(2):
                        g = (s * TT + t) * 2 + h
                        if g >= 4:
                            pe.wait_ge(f_out, g - 3)
                        for f in range(4):
                            ins = pe.transpose(ps[[2, 3, 6, 7][g % 4]][:, f * P:(f + 1) * P],
                                               xt[:, s, 4 * h + f, t * P:(t + 1) * P], ident[:, :])
                        ins.then_inc(f_tr, 1)

            for s in range(NSEQ):
                if s == 0:
                    pe.wait_ge(dn_free, 16 * NPAIR)
                    pe.wait_ge(p_lo, 2)
                else:
                    pe.wait_ge(x3_lo, 2 * KT)
                    turn_p(1)
                    pe.wait_ge(p_lo, 4)
                gate(s, 0, 0)
                pe.wait_ge(sq_sum, 16 + KT * (s + 1))
                sums(6, s).then_inc(ss_ready, 1)
                gate(s, 0, 1)
                spread(B_X3 + s, 7)
                if s == 1:
                    pe.wait_ge(r_copied, 6)
                    pe.wait_ge(x4_ready, KT)
                    turn_x4(0)
                with pe.Fori(1, KT // 2) as i:
                    gate(s, i, 0)
                    gate(s, i, 1)
            pe.wait_ge(x4_ready, 2 * KT)
            turn_x4(1)

        @block.scalar
        def _(act):
            small = [("norm1", 8), ("norm2", 8), ("norm3", 8), ("q_a_norm", 2), ("kv_a_norm", 1), ("pool_scale", 4),
                     ("b_ple_gate", 8)]
            r = 0
            for name, k in small:
                act.dma_start(prow[r:r + k, 2, :], w[name].rearrange("(k p) -> k p", p=P)).then_inc(gains_in, 16)
                r += k
            taps = [w["conv_w"][k] for k in range(3)] + [w["conv_b"]]
            for k in range(4):
                h = (k % 2) * 44
                act.dma_start(prow[h:h + 44, k // 2, :], taps[k].rearrange("(k p) -> k p", p=P)).then_inc(taps_in, 16)

            def x_unit(u):
                s, f = divmod(u, KT)
                act.wait_ge(x_tr, u + 1)
                act.activation(XH[:, s, f, :], ps[4 + u % 3][:, :], ACT.Copy, scale=par[:, N1 + f:N1 + f + 1]).then_inc(x_hi, 1)

            def squares(s):
                for t in range(TT):
                    act.wait_ge(x_in[t], 16 * (s + 1))
                    if s + t:
                        act.wait_ge(x_sq, s * TT + t)
                    act.activation(SF[:, 4096:5120], xtok[:, t, :], ACT.Square,
                                   accum_out=col[:, SSX + s * TT + t:SSX + s * TT + t + 1]).then_inc(x_sq, 1)

            act.wait_ge(par_copied, 1)
            for u in range(KT):
                x_unit(u)
            act.wait_ge(win_in[0], 16)
            act.wait_ge(rot_done, 2)
            split_w_hi(act, 0, None, 0)
            squares(0)
            for u in range(KT, 2 * KT):
                x_unit(u)
            act.wait_ge(win_in[1], 16)
            split_w_hi(act, 1, None, 0)
            squares(1)

            def copy_r(q, bank):
                act.wait_ge(rb_ready, q + 1)
                act.activation(R[:, q % 2, :], ps[bank][:, :], ACT.Copy).then_inc(r_copied, 1)

            copy_r(B_X, 4)
            copy_r(B_X + 1, 5)

            def c_split(c, s):
                act.activation(CHL[:, 0, c, s, :], cs[:, c, s, :], ACT.Copy).then_inc(c_hi, 1)

            for n in range(8):
                if n == 0:
                    for s in range(NSEQ):
                        act.wait_ge(kr_ready, s + 1)
                        for h in range(2):
                            act.activation(KH[NOPE:HEAD, h, s, :], SQ[NOPE:HEAD, s, :], ACT.Copy).then_inc(kr_hi, 1)
                if n + 2 < 8:
                    act.wait_ge(win_in[slot(n)], 16 * ((n + 2) // 2 + 1))
                    split_w_hi(act, n + 2, acc_ready, 2 * (n + 1))
                elif n + 2 == T_POOL:
                    act.wait_ge(poolw_in, 16)
                    split_w_hi(act, T_POOL, acc_ready, 2 * (n + 1), cols=4)
                if n == 3:
                    for s in range(NSEQ):
                        act.wait_ge(c_applied, s + 1)
                        c_split(2, s)
                if n == 5:
                    for c in range(2):
                        for s in range(NSEQ):
                            act.wait_ge(c_applied, 2 + 2 * c + s + 1)
                            c_split(c, s)
            act.wait_ge(acc_ready, 16)
            for q in range(8):
                g, s = divmod(q, 2)
                act.wait_ge(diff_ready, q + 1)
                act.activation(XH[:, s, 4 + g, :], PD[:, s, g, :], ACT.Copy).then_inc(d_hi, 1)
            act.wait_ge(rot_done, 4)
            split_w_hi(act, T_ATT, acc_ready, 16, cols=4)
            for q in range(8):
                g, s = divmod(q, 2)
                act.wait_ge(mix_ready, q + 1)
                act.activation(XH[:, s, 4 + g, :], ps[6 + q % 2][:, :], ACT.Copy,
                               scale=par[:, PSC + g:PSC + g + 1]).then_inc(mix_hi, 1)

            act.wait_ge(wkv_in, 16)
            split_w_hi(act, T_ATT + 1, mix_ready, 8, cols=2)

            def project(i, j):
                h, s = divmod(j, 2)
                act.wait_ge(k_proj, i * 4 + j + 1)
                act.activation(KH[0:NOPE, h, s, :], ps[1][0:NOPE, :], ACT.Copy).then_inc(k_hi, 1)
                act.wait_ge(q_rot, i * 4 + j + 1)
                act.activation(QH[0:HEAD, h, s, :], QF[0:HEAD, j % 2, :], ACT.Copy).then_inc(q_hi, 1)

            def values(i):
                for s in range(NSEQ):
                    act.wait_ge(v_proj, i * 2 + s + 1)
                    act.activation(VB[:, s * TT:(s + 1) * TT, :], ps[6 + s][:, :].rearrange("p (k d) -> p k d", k=TT),
                                   ACT.Copy).then_inc(v_copied, 1)

            def pair(i, last):

                def turned(u):
                    j, t = divmod(u, TT)
                    act.wait_ge(p_tr, i * 16 + u + 1)
                    if t == 0:
                        if j >= 2:
                            act.wait_ge(o_ready, i * 4 + j - 1)
                    act.activation(PT[:, j % 2, :, t * P:(t + 1) * P],
                                   ps[4 + u % 2][:, :].rearrange("p (k q) -> p k q", k=TT), ACT.Copy).then_inc(pt_ready, 1)

                def output(j):
                    h, s = divmod(j, 2)
                    act.wait_ge(o_ready, i * 4 + j + 1)
                    act.activation(XH[h * V_DIM:(h + 1) * V_DIM, s, bass.ds(i, 1), :],
                                   ps[6 + j % 2][h * V_DIM:(h + 1) * V_DIM, :], ACT.Copy).then_inc(o_hi, 1)

                for u in range(4 * TT + 3):
                    if u < 4 * TT:
                        act.wait_ge(max_ready, i * 16 + u + 1)
                        if u >= 3:
                            act.wait_ge(p_tr, i * 16 + u - 2)
                        act.activation(PB[:, u % 3, :], ps[2 + u % 2][:, :], ACT.Exp, bias=col[:, NB + u % 4:NB + u % 4 + 1],
                                       accum_out=col[:, RS + u % 4:RS + u % 4 + 1]).then_inc(exp_done, 1)
                    if u % TT == 1 and u // TT < 3:
                        project(i, u // TT + 1)
                    if 2 <= u < 4 * TT + 2:
                        turned(u - 2)
                    if u == 4 * TT + 1 and not last:
                        project(i + 1, 0)
                    if u >= TT + 2 and (u - TT - 2) % TT == 0:
                        output((u - TT - 2) // TT)
                    if u == 12:
                        if last:
                            act.wait_ge(ring_in[slot(T_OUT)], 16)
                        else:
                            act.wait_ge(rot_done, i * 2 + 6)
                        split_w_hi(act, T_ATT, q_proj, i * 4 + 4, cols=KT if last else 4)
                    if u == 13:
                        if last:
                            act.wait_ge(ring_in[slot(T_OUT + 1)], 16)
                        else:
                            act.wait_ge(wkv_in, i * 16 + 32)
                        split_w_hi(act, T_ATT + 1, k_proj, i * 4 + 4, cols=KT if last else 2)
                if not last:
                    values(i + 1)

            project(0, 0)
            values(0)
            with act.Fori(0, HEADS // 2 - 1) as i:
                pair(i, False)
            pair(HEADS // 2 - 1, True)

            def ring_hi(n, more, free, count):
                act.wait_ge(ring_in[slot(n)], more * 8 + 16 * ((n - T_OUT) // 2 + 1))
                split_w_hi(act, n, free, count)

            def x_hi_of(s, m, g, done):
                act.activation(XH[:, s, bass.ds(m, 1), :], xt[:, s, bass.ds(m, 1), :], ACT.Copy,
                               scale=par[:, bass.ds(g + m, 1)]).then_inc(done, 1)

            for s in range(NSEQ):
                with act.Fori(0, KT // 4) as i:
                    for c in range(4):
                        k = s * KT + c
                        ring_hi(T_OUT + k + 2, i * 4, wo_ready, i * 4 + (k + 1))
                        if s == 1:
                            act.wait_ge(x2_ready, i * 4 + (k + 1))
                            x_hi_of(0, i * 4 + c, N2, x2_hi)
            with act.Fori(0, KT) as m:
                act.wait_ge(x2_ready, m + (KT + 1))
                x_hi_of(1, m, N2, x2_hi)
            copy_r(B_X2, 4)
            copy_r(B_X2 + 1, 5)

            def convolve(i, c):
                f, val = divmod(c, 2)
                for s in range(NSEQ):
                    t, r = i * 8 + (2 * c + s), i * 4 + (2 * f + s)
                    act.wait_ge(u_ready, t + 1)
                    if val:
                        act.wait_ge(silu_done, r + 1)
                    elif f or not isinstance(i, int):
                        act.wait_ge(g_ready, r - 1)
                    tap, bias = (col[:, CP + 2 * (2 * q + val) + f:CP + 2 * (2 * q + val) + f + 1] for q in (1, 3))
                    act.activation(C[:, s, :], U[:, s, 1:S + 1], ACT.Identity, scale=tap, bias=bias).then_inc(tap1, 1)
                for s in range(NSEQ):
                    t, r = i * 8 + (2 * c + s), i * 4 + (2 * f + s)
                    if not val:
                        act.wait_ge(conv_done, t + 1)
                        if f or not isinstance(i, int):
                            act.wait_ge(g_lo, r - 1)
                        act.activation(SG[:, s, :], C[:, s, :], ACT.Silu).then_inc(silu_done, 1)

            def g_split(i, f):
                for s in range(NSEQ):
                    act.wait_ge(g_ready, i * 4 + (2 * f + s + 1))
                    act.activation(GHL[:, 0, f, s, :], SG[:, s, :], ACT.Copy).then_inc(g_hi, 1)

            def mlp(i):
                act.wait_ge(cp_ready, i + 1)
                convolve(i, 0)
                ring_hi(T_UP + 2, i * 4, up_ready, i * 8 + 2)
                convolve(i, 1)
                ring_hi(T_UP + 3, i * 4, up_ready, i * 8 + 4)
                act.wait_ge(dn_ready, i * 16)
                g_split(i, 0)
                act.wait_ge(wd_in, i * 16 + 16)
                act.activation(WDHL[:, 0, :, :], WDR, ACT.Copy).then_inc(wd_hi, 1)
                convolve(i, 2)
                ring_hi(T_UP + 4, i * 4, up_ready, i * 8 + 6)
                convolve(i, 3)
                ring_hi(T_UP + 5, i * 4, up_ready, i * 8 + 8)
                g_split(i, 1)

            mlp(0)
            with act.Fori(1, NPAIR) as i:
                mlp(i)

            def p_split(s):
                for k in range(2):
                    act.wait_ge(p_tr_ready, 2 * s + k + 1)
                    act.activation(PH[:, k, s, :], ps[2 + k][:, :], ACT.Copy).then_inc(p_hi, 1)

            for s in range(NSEQ):
                for m in range(KT):
                    act.wait_ge(dn_free, 16 * (NPAIR - 1) + s * KT + m + 1)
                    act.activation(XH[:, s, m, :], xt[:, s, m, :], ACT.Copy,
                                   scale=par[:, N3 + m:N3 + m + 1]).then_inc(x3_hi, 1)
                if s == 0:
                    p_split(0)

            def ple_hi(i, c, free, count):
                act.wait_ge(ple_in[c], i * 16 + 16)
                act.wait_ge(free, count)
                act.activation(PLH[:, c], PLR[:, c], ACT.Copy).then_inc(pl_hi, 1)

            def gate(s, i, c, more=True):
                k = s * KT + c
                if more:
                    ring_hi(T_GATE + k + 2, i * 2, gate_ready, i * 2 + (k + 1))
                act.wait_ge(gz_ready, i * 2 + (k + 1))
                if s or not isinstance(i, int):
                    act.wait_ge(x4_ready, i * 2 + (k - 1))
                act.activation(GS[c], GZ[:, c, :], ACT.Sigmoid, bias=par[:, bass.ds(i * 2 + (BG + c), 1)]).then_inc(sig_ready, 1)
                if more:
                    ple_hi(i + (s * KT // 2 + 1), c, ple_ready, i * 2 + (k + 1))

            def finish(s):
                for t in range(s * TT, (s + 1) * TT):
                    for h in range(2):
                        g = 2 * t + h
                        act.wait_ge(f_tr, g + 1)
                        if t >= 2 and h == 0:
                            act.wait_ge(out_done[t % 2], 16 * (t // 2))
                        act.activation(OT[:, t % 2, h * S:(h + 1) * S], ps[[2, 3, 6, 7][g % 4]][:, :], ACT.Square,
                                       accum_out=col[:, FS + g:FS + g + 1]).then_inc(f_sq, 1)

            for c in range(2):
                ple_hi(0, c, dn_ready, 16 * NPAIR)
            for s in range(NSEQ):
                if s == 1:
                    p_split(1)
                copy_r(B_X3 + s, 7)
                gate(s, 0, 0)
                gate(s, 0, 1)
                if s == 1:
                    finish(0)
                with act.Fori(1, KT // 2 - s) as i:
                    gate(s, i, 0)
                    gate(s, i, 1)
            for c in range(2):
                gate(1, KT // 2 - 1, c, more=False)
            finish(1)

        @block.vector
        def _(dve):
            def f32(v):
                return v.bitcast(F32)

            dve.memset(ones[:, :], 1.0).then_inc(consts_set, 1)
            dve.memset(col[:, HALF:HALF + 8], -0.5).then_inc(consts_set, 1)
            dve.wait_ge(par_tr, 1)
            dve.tensor_copy(par[:, N1:NPAR], ps[7][:, 0:NPAR - N1]).then_inc(par_copied, 1)
            dve.wait_ge(par_copied, 1)

            def x_unit(u):
                s, f = divmod(u, KT)
                dve.wait_ge(x_hi, u + 1)
                dve.tensor_copy(xt[:, s, f, :], ps[4 + u % 3][:, :])
                dve.scalar_tensor_tensor(XL[:, s, f, :], ps[4 + u % 3][:, :], par[:, N1 + f:N1 + f + 1],
                                         f32(XH[:, s, f, :]), ALU.mult, ALU.subtract).then_inc(x_split, 1)

            for u in range(KT):
                x_unit(u)
            dve.wait_ge(par_tr, 2)
            dve.tensor_copy(par[:, 0:N1], ps[7][:, 0:N1]).then_inc(par_copied, 1)
            split_w_lo(dve, 0, 0)
            for u in range(KT, 2 * KT):
                x_unit(u)
            split_w_lo(dve, 1, 1)

            def mean(out, total, n, done=None):
                dve.tensor_scalar(out, total, 1.0 / n, EPS, ALU.mult, ALU.add).then_inc(done, 1)

            def diagonal(q, cols):
                dve.wait_ge(col_ready, cols)
                if q:
                    dve.wait_ge(rb_ready, q)
                for t in range(TT):
                    ins = dve.tensor_scalar(diag[:, t, :], ident[:, :], col[:, R_COL + 4 * q + t:R_COL + 4 * q + t + 1], None, ALU.mult)
                ins.then_inc(diag_ready, 1)

            dve.wait_ge(x_sq, 2 * TT)
            mean(col[:, V_COL:V_COL + 8], col[:, SSX:SSX + 8], D, v_ready)
            diagonal(B_X, 1)
            diagonal(B_X + 1, 1)
            for s in range(NSEQ):
                dve.memset(ub[:, s, 0:PAD], 0.0)
                ins = dve.memset(ub[:, s, PAD + S:UB], 0.0)
            ins.then_inc(pads_zero, 1)
            dve.wait_ge(tabs_in, 32)
            n_chain = 0

            def times_r(n, s, out):
                dve.wait_ge(r_copied, s + 1)
                dve.wait_ge(acc_ready, 2 * n + s + 1)
                return dve.tensor_tensor(out, ps[2 * (n % 2) + s][:, :], R[:, s, :], ALU.mult).then_inc(acc_free, 1)

            for n in range(8):
                if n == 0:
                    for s in range(NSEQ):
                        kr = (w1, w2)[s][:, 0:S]
                        times_r(n, s, kr)
                        dve.wait_ge(acc_free, s + 1)
                        if s:
                            dve.wait_ge(kr_ready, s)
                        dve.tensor_tensor(SQT[NOPE:HEAD, :], kr[HEAD:P, :], tab_k[HEAD:P, :], ALU.mult).then_inc(kr_step, 1)
                        dve.tensor_tensor(SQ[NOPE:HEAD, s, :], kr[NOPE:HEAD, :], tab_k[NOPE:HEAD, :], ALU.mult).then_inc(kr_step, 1)
                        dve.wait_ge(kr_step, 2 * s + 2)
                        dve.tensor_tensor(SQ[NOPE:HEAD, s, :], SQ[NOPE:HEAD, s, :], SQT[NOPE:HEAD, :], ALU.add).then_inc(kr_ready, 1)
                    for s in range(NSEQ):
                        for h in range(2):
                            dve.wait_ge(kr_hi, 2 * s + h + 1)
                            dve.tensor_tensor(KL[NOPE:HEAD, h, s, :], SQ[NOPE:HEAD, s, :], f32(KH[NOPE:HEAD, h, s, :]),
                                              ALU.subtract).then_inc(kr_done, 1)
                elif n < 4:
                    c = (2, 0, 1)[n - 1]
                    if n == 1:
                        dve.wait_ge(xt_spilled, 16)
                    for s in range(NSEQ):
                        times_r(n, s, cs[:, c, s, :])
                        dve.wait_ge(acc_free, 2 * n + s + 1)
                else:
                    g = n - 4
                    if n == 4:
                        dve.wait_ge(pads_zero, 1)
                        dve.wait_ge(edge_in, 16)
                    for s in range(NSEQ):
                        if n_chain:
                            dve.wait_ge(diff_ready, (n - 4) * 2 + s)
                        u = ub[:, s, :]
                        times_r(n, s, u[:, PAD:PAD + S])
                        dve.wait_ge(acc_free, 2 * n + s + 1)
                        cur, lo, hi = u, 0, UB
                        for k in range(g + 1):
                            left, right = (1, 0) if k == 0 else (1 << (k - 1), 1 << (k - 1))
                            lo, hi = lo + left, hi - right
                            nxt = (w1, w2)[k % 2]
                            dve.tensor_tensor(nxt[:, lo:hi], cur[:, lo - left:hi - left], cur[:, lo + right:hi + right],
                                              ALU.add).then_inc(chain, 1)
                            n_chain += 1
                            dve.wait_ge(chain, n_chain)
                            cur = nxt
                        dve.scalar_tensor_tensor(PD[:, s, g, :], cur[:, PAD:PAD + S], 1.0 / POOL_WINDOWS[g], u[:, PAD:PAD + S],
                                                 ALU.mult, ALU.subtract).then_inc(chain, 1)
                        dve.tensor_tensor(col[:, CP:CP + PAD], cur[:, PAD:2 * PAD], edge[:, g, 0:PAD], ALU.mult).then_inc(chain, 1)
                        dve.tensor_tensor(col[:, CP + PAD:CP + 2 * PAD], cur[:, S:S + PAD], edge[:, g, PAD:2 * PAD],
                                          ALU.mult).then_inc(chain, 1)
                        n_chain += 3
                        dve.wait_ge(chain, n_chain)
                        dve.tensor_tensor(PD[:, s, g, 0:PAD], col[:, CP:CP + PAD], u[:, PAD:2 * PAD], ALU.subtract)
                        dve.tensor_tensor(PD[:, s, g, S - PAD:S], col[:, CP + PAD:CP + 2 * PAD], u[:, S:S + PAD],
                                          ALU.subtract).then_inc(diff_ready, 1)
                if n == 2:
                    dve.wait_ge(ss_ready, 1)
                    mean(col[:, V_COL + 8:V_COL + 16], ps[6][:, 0:8], KV_RANK, v_ready)
                    diagonal(B_KV, 2)
                if n == 4:
                    dve.wait_ge(ss_ready, 2)
                    mean(col[:, V_COL + 16:V_COL + 24], ps[6][:, 0:8], Q_RANK, v_ready)
                    diagonal(B_Q, 3)
                if n + 2 <= T_POOL:
                    split_w_lo(dve, n + 2, n + 2, cols=KT if n + 2 < T_POOL else 4)
                if n == 3:
                    diagonal(B_KV + 1, 2)
                    for s in range(NSEQ):
                        dve.wait_ge(rb_ready, B_KV + s + 1)
                        dve.scalar_tensor_tensor(cs[:, 2, s, :], cs[:, 2, s, :], par[:, GKV:GKV + 1], ps[4 + s][:, :],
                                                 ALU.mult, ALU.mult).then_inc(c_applied, 1)
                    for s in range(NSEQ):
                        dve.wait_ge(c_hi, s + 1)
                        dve.tensor_tensor(CHL[:, 1, 2, s, :], cs[:, 2, s, :], f32(CHL[:, 0, 2, s, :]), ALU.subtract).then_inc(c_lo, 1)
                if n == 5:
                    diagonal(B_Q + 1, 3)
                    dve.wait_ge(rb_ready, B_Q + 2)
                    for c in range(2):
                        for s in range(NSEQ):
                            dve.scalar_tensor_tensor(cs[:, c, s, :], cs[:, c, s, :], par[:, GQ + c:GQ + c + 1], ps[4 + s][:, :],
                                                     ALU.mult, ALU.mult).then_inc(c_applied, 1)
                    for c in range(2):
                        for s in range(NSEQ):
                            dve.wait_ge(c_hi, 2 + 2 * c + s + 1)
                            dve.tensor_tensor(CHL[:, 1, c, s, :], cs[:, c, s, :], f32(CHL[:, 0, c, s, :]),
                                              ALU.subtract).then_inc(c_lo, 1)
            for q in range(8):
                g, s = divmod(q, 2)
                dve.wait_ge(d_hi, q + 1)
                dve.tensor_tensor(XL[:, s, 4 + g, :], PD[:, s, g, :], f32(XH[:, s, 4 + g, :]), ALU.subtract).then_inc(d_lo, 1)
            split_w_lo(dve, T_ATT, T_ATT, cols=4)
            for q in range(8):
                g, s = divmod(q, 2)
                dve.wait_ge(mix_hi, q + 1)
                dve.scalar_tensor_tensor(XL[:, s, 4 + g, :], ps[6 + q % 2][:, :], par[:, PSC + g:PSC + g + 1],
                                         f32(XH[:, s, 4 + g, :]), ALU.mult, ALU.subtract).then_inc(mix_lo, 1)
            split_w_lo(dve, T_ATT + 1, T_ATT + 1, cols=2)

            def rotate(i, j):
                dve.wait_ge(q_proj, i * 4 + j + 1)
                if not isinstance(i, int) or i or j:
                    dve.wait_ge(q_rot, i * 4 + j)
                dve.tensor_tensor(QF[0:HEAD, j % 2, :], ps[0][0:HEAD, :], tab_q[0:HEAD, :], ALU.mult).then_inc(q_step, 1)
                dve.tensor_tensor(QTMP[NOPE:HEAD, :], ps[0][HEAD:P, :], tab_q[HEAD:P, :], ALU.mult).then_inc(qf_ready, 1)
                dve.wait_ge(q_step, i * 4 + j + 1)
                dve.wait_ge(qf_ready, i * 4 + j + 1)
                dve.tensor_tensor(QF[NOPE:HEAD, j % 2, :], QF[NOPE:HEAD, j % 2, :], QTMP[NOPE:HEAD, :],
                                  ALU.add).then_inc(q_rot, 1)

            def lows(i, j):
                h, s = divmod(j, 2)
                dve.wait_ge(k_hi, i * 4 + j + 1)
                dve.tensor_tensor(KL[0:NOPE, h, s, :], ps[1][0:NOPE, :], f32(KH[0:NOPE, h, s, :]), ALU.subtract).then_inc(k_lo, 1)
                dve.wait_ge(q_hi, i * 4 + j + 1)
                dve.tensor_tensor(QL[0:HEAD, h, s, :], QF[0:HEAD, j % 2, :], f32(QH[0:HEAD, h, s, :]),
                                  ALU.subtract).then_inc(q_lo, 1)

            def pair(i, last):
                def normalise(u):
                    dve.wait_ge(exp_done, i * 16 + u + 1)
                    dve.reciprocal(col[:, RC + u % 4:RC + u % 4 + 1], col[:, RS + u % 4:RS + u % 4 + 1]).then_inc(rc_ready, 1)
                    dve.wait_ge(rc_ready, i * 16 + u + 1)
                    dve.tensor_scalar(PB[:, u % 3, :], PB[:, u % 3, :], col[:, RC + u % 4:RC + u % 4 + 1], None,
                                      ALU.mult).then_inc(p_norm, 1)

                for u in range(4 * TT + 3):
                    if u < 4 * TT:
                        dve.wait_ge(s_ready, i * 16 + u + 1)
                        dve.tensor_reduce(col[:, NB + u % 4:NB + u % 4 + 1], ps[2 + u % 2][:, :], AX_X, ALU.max,
                                          negate=True).then_inc(max_ready, 1)
                    if u and u <= 4 * TT:
                        normalise(u - 1)
                    if u % TT == 1 and u // TT < 3:
                        rotate(i, u // TT + 1)
                    if u % TT == 2 and u // TT < 3:
                        lows(i, u // TT + 1)
                    if u == 4 * TT + 1 and not last:
                        rotate(i + 1, 0)
                    if u == 4 * TT + 2 and not last:
                        lows(i + 1, 0)
                    if u >= TT + 2 and (u - TT - 2) % TT == 0:
                        j = (u - TT - 2) // TT
                        h, s = divmod(j, 2)
                        rows = slice(h * V_DIM, (h + 1) * V_DIM)
                        dve.wait_ge(o_hi, i * 4 + j + 1)
                        dve.tensor_tensor(XL[rows, s, bass.ds(i, 1), :], ps[6 + j % 2][rows, :],
                                          f32(XH[rows, s, bass.ds(i, 1), :]), ALU.subtract).then_inc(o_lo, 1)
                    if u == 12:
                        split_w_lo(dve, T_ATT, i * 2 + (T_ATT + 2), cols=KT if last else 4)
                    if u == 13:
                        split_w_lo(dve, T_ATT + 1, i * 2 + (T_ATT + 3), cols=KT if last else 2)

            rotate(0, 0)
            lows(0, 0)
            with dve.Fori(0, HEADS // 2 - 1) as i:
                pair(i, False)
            pair(HEADS // 2 - 1, True)

            def x_lo_of(s, m, g, hi, count, done):
                dve.wait_ge(hi, count)
                dve.scalar_tensor_tensor(XL[:, s, bass.ds(m, 1), :], xt[:, s, bass.ds(m, 1), :], par[:, bass.ds(g + m, 1)],
                                         f32(XH[:, s, bass.ds(m, 1), :]), ALU.mult, ALU.subtract).then_inc(done, 1)

            for s in range(NSEQ):
                for h in range(2):
                    dve.wait_ge(xt_back[2 * s + h], 16)
                with dve.Fori(0, KT // 4) as i:
                    for c in range(4):
                        k = s * KT + c
                        dve.wait_ge(wo_ready, i * 4 + (k + 1))
                        dve.tensor_tensor(xt[:, s, bass.ds(i * 4 + c, 1), :], xt[:, s, bass.ds(i * 4 + c, 1), :], ps[c][:, :],
                                          ALU.add).then_inc(x2_ready, 1)
                        split_w_lo(dve, T_OUT + k + 2, i * 4 + (T_OUT + k + 2))
                        if s == 1:
                            x_lo_of(0, i * 4 + c, N2, x2_hi, i * 4 + (c + 1), x2_lo)
            with dve.Fori(0, KT) as m:
                x_lo_of(1, m, N2, x2_hi, m + (KT + 1), x2_lo)

            dve.wait_ge(ss_ready, 3)
            mean(col[:, V_COL + 24:V_COL + 32], ps[6][:, 0:8], D, v_ready)
            diagonal(B_X2, 4)
            for s in range(NSEQ):
                dve.memset(U[:, s, 0:1], 0.0)
                ins = dve.memset(U[:, s, S + 1:S + 2], 0.0)
            ins.then_inc(u_pads, 1)
            diagonal(B_X2 + 1, 4)

            def scaled(i, c, s):
                t = i * 8 + (2 * c + s)
                dve.wait_ge(up_ready, t + 1)
                if c or not isinstance(i, int):
                    dve.wait_ge(conv_done, t - 1)
                dve.tensor_tensor(U[:, s, 1:S + 1], ps[2 * (c % 2) + s][:, :], R[:, s, :], ALU.mult).then_inc(u_ready, 1)

            def taps(i, c):
                f, val = divmod(c, 2)
                tap_l, tap_r = (col[:, CP + 2 * (2 * q + val) + f:CP + 2 * (2 * q + val) + f + 1] for q in (0, 2))
                for s in range(NSEQ):
                    t = i * 8 + (2 * c + s)
                    dve.wait_ge(tap1, t + 1)
                    dve.scalar_tensor_tensor(C[:, s, :], U[:, s, 0:S], tap_l, C[:, s, :], ALU.mult, ALU.add).then_inc(tap0, 1)
                for s in range(NSEQ):
                    t = i * 8 + (2 * c + s)
                    dve.wait_ge(tap0, t + 1)
                    dve.scalar_tensor_tensor(C[:, s, :], U[:, s, 2:S + 2], tap_r, C[:, s, :], ALU.mult, ALU.add).then_inc(conv_done, 1)

            def product(i, f):
                for s in range(NSEQ):
                    r = i * 4 + (2 * f + s)
                    dve.wait_ge(silu_done, r + 1)
                    dve.wait_ge(conv_done, i * 8 + (2 * (2 * f + 1) + s + 1))
                    dve.tensor_tensor(SG[:, s, :], SG[:, s, :], C[:, s, :], ALU.mult).then_inc(g_ready, 1)

            def g_lows(i, f):
                for s in range(NSEQ):
                    dve.wait_ge(g_hi, i * 4 + (2 * f + s + 1))
                    dve.tensor_tensor(GHL[:, 1, f, s, :], SG[:, s, :], f32(GHL[:, 0, f, s, :]), ALU.subtract).then_inc(g_lo, 1)

            def add_down(i, s, m):
                g = s * KT + m
                dve.wait_ge(dn_ready, i * 16 + (g + 1))
                dve.tensor_tensor(xt[:, s, m, :], xt[:, s, m, :], ps[4 + g % 4][:, :], ALU.add).then_inc(dn_free, 1)

            def mlp(i, first):
                for c in range(4):
                    f, val = divmod(c, 2)
                    for s in range(NSEQ):
                        if first and c == 0:
                            dve.wait_ge(r_copied, s + 3)
                        scaled(i, c, s)
                    taps(i, c)
                    if val:
                        product(i, f)
                    split_w_lo(dve, T_UP + c + 2, i * 4 + (T_UP + c + 2))
                    if c == 1:
                        if not first:
                            for s in range(NSEQ):
                                for m in range(KT):
                                    add_down(i - 1, s, m)
                        g_lows(i, 0)
                        dve.wait_ge(wd_hi, i + 1)
                        dve.tensor_tensor(WDHL[:, 1, :, :], WDR, f32(WDHL[:, 0, :, :]), ALU.subtract).then_inc(wd_lo, 1)
                    if c == 3:
                        g_lows(i, 1)

            dve.wait_ge(u_pads, 1)
            mlp(0, True)
            with dve.Fori(1, NPAIR) as i:
                mlp(i, False)

            def p_lows(s):
                for k in range(2):
                    dve.wait_ge(p_hi, 2 * s + k + 1)
                    dve.tensor_tensor(PL[:, k, s, :], ps[2 + k][:, :], f32(PH[:, k, s, :]), ALU.subtract).then_inc(p_lo, 1)

            def x3_low(k):
                s, m = divmod(k, KT)
                dve.wait_ge(x3_hi, k + 1)
                dve.scalar_tensor_tensor(XL[:, s, m, :], xt[:, s, m, :], par[:, N3 + m:N3 + m + 1], f32(XH[:, s, m, :]),
                                         ALU.mult, ALU.subtract).then_inc(x3_lo, 1)

            for k in range(2 * KT):
                add_down(NPAIR - 1, k // KT, k % KT)
                if k:
                    x3_low(k - 1)
                if k == KT:
                    p_lows(0)
            x3_low(2 * KT - 1)

            def ple_low(i, c):
                dve.wait_ge(pl_hi, i * 2 + (c + 1))
                dve.tensor_tensor(PLL[:, c], PLR[:, c], f32(PLH[:, c]), ALU.subtract).then_inc(pl_lo, 1)

            def gate(s, i, c, more=True):
                k = s * KT + c
                m = i * 2 + c
                dve.wait_ge(gate_ready, i * 2 + (k + 1))
                if s or not isinstance(i, int):
                    dve.wait_ge(sig_ready, i * 2 + (k - 1))
                dve.tensor_tensor(GZ[:, c, :], ps[c][:, :], R[:, s, :], ALU.mult).then_inc(gz_ready, 1)
                if more:
                    split_w_lo(dve, T_GATE + k + 2, i * 2 + (T_GATE + k + 2))
                dve.wait_ge(ple_ready, i * 2 + (k + 1))
                dve.wait_ge(sig_ready, i * 2 + (k + 1))
                dve.tensor_tensor(GS[c], ps[4 + c][:, :], GS[c], ALU.mult).then_inc(gp_ready, 1)
                dve.wait_ge(gp_ready, i * 2 + (k + 1))
                dve.tensor_tensor(xt[:, s, bass.ds(m, 1), :], xt[:, s, bass.ds(m, 1), :], GS[c], ALU.add).then_inc(x4_ready, 1)
                if more:
                    ple_low(i + (s * KT // 2 + 1), c)

            def finish(s):
                def stats(t):
                    dve.wait_ge(f_sq, 2 * t + 2)
                    dve.tensor_tensor(col[:, FV + t:FV + t + 1], col[:, FS + 2 * t:FS + 2 * t + 1],
                                      col[:, FS + 2 * t + 1:FS + 2 * t + 2], ALU.add).then_inc(f_sum, 1)
                    dve.wait_ge(f_sum, t + 1)
                    mean(col[:, FV + t:FV + t + 1], col[:, FV + t:FV + t + 1], D, f_v)

                stats(s * TT)
                for t in range(s * TT, (s + 1) * TT):
                    if (t + 1) % TT:
                        stats(t + 1)
                    dve.wait_ge(f_r, t + 1)
                    for h in range(2):
                        cols = slice(h * S, (h + 1) * S)
                        dve.scalar_tensor_tensor(OT[:, t % 2, cols], ps[[2, 3, 6, 7][(2 * t + h) % 4]][:, :],
                                                 col[:, FR + t:FR + t + 1], gain_row[:, cols], ALU.mult, ALU.mult).then_inc(f_out, 1)

            for c in range(2):
                ple_low(0, c)
            for s in range(NSEQ):
                if s == 1:
                    p_lows(1)
                dve.wait_ge(ss_ready, 4 + s)
                mean(col[:, V_COL + 32 + 4 * s:V_COL + 36 + 4 * s], ps[6][:, 4 * s:4 * s + 4], D, v_ready)
                diagonal(B_X3 + s, 5 + s)
                dve.wait_ge(r_copied, B_X3 - 4 + s + 1)
                gate(s, 0, 0)
                gate(s, 0, 1)
                if s == 1:
                    dve.wait_ge(row_in, 16)
                    finish(0)
                with dve.Fori(1, KT // 2 - s) as i:
                    gate(s, i, 0)
                    gate(s, i, 1)
            for c in range(2):
                gate(1, KT // 2 - 1, c, more=False)
            finish(1)

        @block.gpsimd
        def _(pool):
            def rot_columns(n, k):
                q = ROPE // 2
                pool.tensor_scalar(WR[:, slot(n), 0:k, HEAD:HEAD + q], WR[:, slot(n), 0:k, HEAD - q:HEAD], -1.0, 1.0,
                                   ALU.mult, ALU.mult).then_inc(rot_done, 1)
                pool.tensor_copy(WR[:, slot(n), 0:k, HEAD + q:P], WR[:, slot(n), 0:k, NOPE:NOPE + q]).then_inc(rot_done, 1)

            def root(q, n, count):
                pool.wait_ge(v_ready, count)
                pool.tensor_tensor(col[:, R_COL + 4 * q:R_COL + 4 * q + n], col[:, V_COL + 4 * q:V_COL + 4 * q + n],
                                   col[:, HALF:HALF + n], ALU.pow).then_inc(col_ready, 1)

            pool.wait_ge(win_in[0], 16)
            rot_columns(T_IN, KT)
            pool.wait_ge(consts_set, 2)
            root(B_X, 8, 1)
            pool.wait_ge(kr_done, 4)
            for s in range(NSEQ):
                pool.wait_ge(acc_free, 2 + s + 1)
                pool.tensor_tensor(SQ[:, s, :], cs[:, 2, s, :], cs[:, 2, s, :], ALU.mult).then_inc(sq_ready, 1)
            root(B_KV, 8, 2)
            for s in range(NSEQ):
                pool.wait_ge(acc_free, 6 + s + 1)
                pool.tensor_tensor(SQ[:, s, :], cs[:, 0, s, :], cs[:, 0, s, :], ALU.mult).then_inc(sq_part, 1)
                if s:
                    pool.wait_ge(sq_ready, 3)
                pool.tensor_tensor(SQT, cs[:, 1, s, :], cs[:, 1, s, :], ALU.mult).then_inc(sq_part, 1)
                pool.wait_ge(sq_part, 2 * s + 2)
                pool.tensor_tensor(SQ[:, s, :], SQ[:, s, :], SQT, ALU.add).then_inc(sq_ready, 1)
            root(B_Q, 8, 3)
            pool.wait_ge(wq_in, 32)
            rot_columns(T_ATT, 4)

            for i in range(1, HEADS // 2):
                pool.wait_ge(wq_in, i * 32 + 32)
                rot_columns(T_ATT, 4)

            def squares(s, m, ready, count, done):
                pool.wait_ge(ready, count)
                pool.tensor_tensor(SQT, xt[:, s, bass.ds(m, 1), :], xt[:, s, bass.ds(m, 1), :], ALU.mult).then_inc(sq_mul, 1)
                pool.wait_ge(sq_mul, done)
                pool.tensor_tensor(SQ[:, s, :], SQ[:, s, :], SQT, ALU.add).then_inc(sq_sum, 1)
                pool.wait_ge(sq_sum, done)

            pool.memset(SQ[:, :, :], 0.0).then_inc(sq_zero, 1)
            pool.wait_ge(sq_zero, 1)
            for s in range(NSEQ):
                with pool.Fori(0, KT) as m:
                    squares(s, m, x2_ready, m + (s * KT + 1), m + (s * KT + 1))
            root(B_X2, 8, 4)

            def place_taps(i, first=False):
                if not first:
                    pool.wait_ge(conv_done, i * 8)
                pool.tensor_copy(col[:, CP:CP + 16].rearrange("p (k f) -> p k f", f=2),
                                 par[:, 0:N1].rearrange("p (k f) -> p k f", f=FT)[:, :, bass.ds(i * 2, 2)]).then_inc(cp_ready, 1)

            place_taps(0, first=True)
            with pool.Fori(1, NPAIR) as i:
                place_taps(i)

            pool.wait_ge(g_ready, 4 * NPAIR)
            pool.memset(SQ[:, :, :], 0.0).then_inc(sq_zero, 1)
            pool.wait_ge(sq_zero, 2)
            for s in range(NSEQ):
                with pool.Fori(0, KT) as m:
                    squares(s, m, dn_free, m + (16 * (NPAIR - 1) + s * KT + 1), m + (2 * KT + s * KT + 1))
                if s == 0:
                    root(B_X3, 4, 5)
            root(B_X3 + 1, 4, 6)
            for t in range(NSEQ * TT):
                pool.wait_ge(f_v, t + 1)
                pool.tensor_tensor(col[:, FR + t:FR + t + 1], col[:, FV + t:FV + t + 1], col[:, HALF:HALF + 1],
                                   ALU.pow).then_inc(f_r, 1)


_WEIGHTS = ["norm1", "w_in", "q_a_norm", "w_q_b", "kv_a_norm", "w_kv_b", "pool_w", "pool_scale", "w_out", "norm2",
            "w_up", "conv_w", "conv_b", "w_down", "norm3", "w_ple_gate", "b_ple_gate", "w_ple_proj", "final_norm"]


def _constants():
    inv = 1.0 / (10000.0 ** (np.arange(0, ROPE, 2, dtype=np.float32) / ROPE))
    ang = np.arange(S, dtype=np.float32)[:, None] * inv[None, :]
    emb = np.concatenate([ang, ang], axis=-1).T
    cos, sin = np.cos(emb).astype(np.float32), np.sin(emb).astype(np.float32)
    scale = np.float32(HEAD ** -0.5)
    rope_k = np.concatenate([np.ones((NOPE, S), np.float32), cos, sin])
    edge = np.zeros((4, 2 * PAD), np.float32)
    t = np.concatenate([np.arange(PAD), np.arange(S - PAD, S)])
    for g, w in enumerate(POOL_WINDOWS):
        edge[g] = 1.0 / (np.clip(t - w // 2 + w, 0, S) - np.clip(t - w // 2, 0, S)).astype(np.float32)
    return {"ident": np.eye(P, dtype=np.float32), "rope_k": rope_k, "rope_q": rope_k * scale, "pool_edge": edge}


def kernel(**inputs):
    import concourse.bacc as _bacc
    from concourse.bass_utils import run_bass_kernel_spmd as _run

    nc = _bacc.Bacc("TRN2", target_bir_lowering=False, num_devices=1)
    arrays = {}

    def dram(name, a):
        a = np.ascontiguousarray(a)
        arrays[f"in_{name}"] = a
        return nc.dram_tensor(f"in_{name}", a.shape, mybir.dt.from_np(a.dtype), kind="ExternalInput").ap()

    x = [dram(n, np.asarray(inputs[n])[0]) for n in ("x_prompt", "x_sample")]
    p_in = [dram(n, np.asarray(inputs[n])[0, 0]) for n in ("p_prompt", "p_sample")]
    w = {n: dram(n, np.asarray(inputs[n])[0] if n != "final_norm" else np.asarray(inputs[n])) for n in _WEIGHTS}
    consts = {n: dram(n, a) for n, a in _constants().items()}
    y = [nc.dram_tensor(f"out_{i}", (S, D), F32, kind="ExternalOutput").ap() for i in range(NSEQ)]
    encoder(nc, x, p_in, w, y, consts)
    r = _run(nc, [arrays], core_ids=[0])
    return tuple(r.results[0][f"out_{i}"].reshape(1, S, D) for i in range(NSEQ))
```

```python
from contextlib import ExitStack

import numpy as np

import concourse.bass as bass
from concourse import mybir

F32 = mybir.dt.float32
F32R = mybir.dt.float32r
ACT = mybir.ActivationFunctionType
ALU = mybir.AluOpType
AX_X = mybir.AxisListType.X

P = 128
D = 1024
S = 512
NSEQ = 2
KT = D // P
TT = S // P
Q_RANK, KV_RANK, ROPE, NOPE, V_DIM, HEADS = 256, 128, 32, 64, 64, 8
HEAD = NOPE + ROPE
POOL_WINDOWS = (2, 4, 8, 16)
PAD = 8
UB = S + 2 * PAD
FF = 2816
FT = FF // P
NPAIR = FT // 2
EPS = 1e-6

N1 = 4 * 2 * FT
N2, N3, GQ = N1 + KT, N1 + 2 * KT, N1 + 3 * KT
GKV, PSC, BG = GQ + 2, GQ + 3, GQ + 7
NPAR = BG + KT

T_IN, T_POOL, T_ATT, T_OUT = 0, 8, 9, 17
T_UP = T_OUT + NSEQ * KT
T_GATE = T_UP + 4 * NPAIR

B_X, B_KV, B_Q, B_X2, B_X3 = 0, 2, 4, 6, 8


def encoder(nc, x, p_in, w, y, consts):
    with ExitStack() as ctx:
        def sb(name, shape, dt=F32):
            return ctx.enter_context(nc.sbuf_tensor(name, shape, dt))

        def sem(name):
            return ctx.enter_context(nc.semaphore(name))

        XT = sb("XT", [P, NSEQ * KT * S])
        XH = sb("XH", [P, NSEQ, KT, S], F32R)
        XL = sb("XL", [P, NSEQ, KT, S], F32R)
        xt = XT[:, :].rearrange("p (s k t) -> p s k t", s=NSEQ, k=KT)
        R = sb("R", [P, NSEQ, S])
        ident = sb("ident", [P, P])
        ones = sb("ones", [P, P])
        par = sb("par", [P, NPAR])
        WR = sb("WR", [P, 2, KT, P])
        WH = sb("WH", [P, 2, KT, P], F32R)
        WL = sb("WL", [P, 2, KT, P], F32R)
        diag = sb("diag", [P, TT, P])
        edge = sb("edge", [P, 4, 2 * PAD])
        V_COL, R_COL, SSX, NB, RS, RC, FS, FV, FR, HALF, CP = 0, 40, 80, 88, 92, 96, 100, 116, 124, 132, 140
        col = sb("col", [P, CP + 32])
        SF = sb("SF", [P, 5124])
        with ExitStack() as tail:
            TL = tail.enter_context(nc.sbuf_tensor("TL", [P, 4 * D], F32))
        GHL = sb("GHL", [P, 2, 2, NSEQ, S], F32R)
        WDHL = sb("WDHL", [P, 2, 2, D], F32R)
        CHL = sb("CHL", [P, 2, 3, NSEQ, S], F32R)

        xtok = [v.rearrange("p (a d) -> p a d", a=TT) for v in (SF[:, 0:TT * D], TL[:, :])]
        prow = XT[:, 8192 - 512:8192 - 128].rearrange("p (a d) -> p a d", a=3)
        SQ = SF[:, 0:1024].rearrange("p (s t) -> p s t", s=NSEQ)
        SQT = SF[:, 1028:1540]
        ub = SF[:, 1540:1540 + 2 * UB].rearrange("p (s t) -> p s t", s=NSEQ)
        w1, w2 = SF[:, 2596:2596 + UB], SF[:, 3124:3124 + UB]
        win = [(w1, w2), (TL[:, D:D + UB], TL[:, 3 * D:3 * D + UB])]
        tab_q, tab_k = SF[:, 4096:4608], SF[:, 4608:5120]
        PD = XT[:, 0:4096].rearrange("p (s g t) -> p s g t", s=NSEQ, g=4)
        cs = XT[:, 4096:7168].rearrange("p (c s t) -> p c s t", c=3, s=NSEQ)
        PT = XT[:, 0:4096].rearrange("p (a k q) -> p a k q", a=2, k=TT)
        PB = XT[:, 4096:6144].rearrange("p (a k) -> p a k", a=4)
        VB = XT[:, 6144:7168].rearrange("p (k d) -> p k d", d=P)
        QF = XT[:, 7168:8192].rearrange("p (a t) -> p a t", a=2)
        QTMP = SQT
        QH, QL = GHL[:, 0], GHL[:, 1]
        KH = WDHL[:, 0].rearrange("p h (s t) -> p h s t", s=NSEQ)
        KL = WDHL[:, 1].rearrange("p h (s t) -> p h s t", s=NSEQ)
        U = SF[:, 0:1028].rearrange("p (s t) -> p s t", s=NSEQ)
        C = SF[:, 1028:2052].rearrange("p (s t) -> p s t", s=NSEQ)
        SG = SF[:, 2052:3076].rearrange("p (s t) -> p s t", s=NSEQ)
        WDR = SF[:, 3076:5124].rearrange("p (k m) -> p k m", k=2)
        sq3 = [SQT, SF[:, 1540:2052]]
        ptok = SF[:, 2052:3076].rearrange("p (t d) -> p t d", t=TT)
        PLR = SF[:, 3076:3588].rearrange("p (a k m) -> p a k m", a=2, k=2)
        GZ = SF[:, 3588:4612].rearrange("p (a t) -> p a t", a=2)
        GS = [SF[:, 4612:5124], SF[:, 1540:2052]]
        PLH = WDHL[:, 0].rearrange("p k (a m) -> p a k m", m=P)
        PLL = WDHL[:, 1].rearrange("p k (a m) -> p a k m", m=P)
        PH, PL = CHL[:, 0], CHL[:, 1]
        gain_row = TL[:, 0:D]
        OT = TL[:, D:4 * D].rearrange("p (a d) -> p a d", a=3)

        ps = [ctx.enter_context(nc.psum_tensor(f"ps{b}", [P, 512], F32)) for b in range(8)]
        xt_dram = nc.dram_tensor("xt_scratch", (P, NSEQ * KT * S), F32, kind="Internal").ap()

        ident_in, gains_in, taps_in, tabs_in, edge_in, row_in = (sem(n) for n in (
            "ident_in", "gains_in", "taps_in", "tabs_in", "edge_in", "row_in"))
        x_in = [sem(f"x_in{i}") for i in range(2 * TT)]
        win_in = [sem(f"win_in{i}") for i in range(2)]
        ring_in = [sem(f"ring_in{i}") for i in range(2)]
        poolw_in, wq_in, wkv_in = sem("poolw_in"), sem("wq_in"), sem("wkv_in")
        ple_in = [sem(f"ple_in{i}") for i in range(2)]
        wd_in, p_in_sem = sem("wd_in"), sem("p_tokens_in")
        xt_spilled = [sem(f"xt_spilled{i}") for i in range(2)]
        xt_back = [sem(f"xt_back{i}") for i in range(4)]
        out_done = [sem(f"out_done{i}") for i in range(3)]
        w_hi, w_lo, rot_done = sem("w_hi"), sem("w_lo"), sem("rot_done")
        consts_set, par_tr, par_copied = sem("consts_set"), sem("par_tr"), sem("par_copied")
        x_tr, x_hi, x_split, x_sq = sem("x_tr"), sem("x_hi"), sem("x_split"), sem("x_sq")
        v_ready, col_ready, diag_ready, rb_ready = sem("v_ready"), sem("col_ready"), sem("diag_ready"), sem("rb_ready")
        r_copied, sq_ready, ss_ready = sem("r_copied"), sem("sq_ready"), sem("ss_ready")
        acc_ready, acc_free = sem("acc_ready"), sem("acc_free")
        kr_step, kr_ready, kr_hi, kr_done = sem("kr_step"), sem("kr_ready"), sem("kr_hi"), sem("kr_done")
        c_applied, c_hi, c_lo = sem("c_applied"), sem("c_hi"), sem("c_lo")
        sq_part, pads_zero = sem("sq_part"), sem("pads_zero")
        chain, diff_ready = ([sem(f"{n}{s}") for s in range(NSEQ)] for n in ("window_steps", "diff_ready"))
        d_hi, d_lo, mix_ready, mix_hi, mix_lo = sem("d_hi"), sem("d_lo"), sem("mix_ready"), sem("mix_hi"), sem("mix_lo")
        q_proj, k_proj, v_proj, v_copied = sem("q_proj"), sem("k_proj"), sem("v_proj"), sem("v_copied")
        q_step, q_rot, qf_ready, q_hi, q_lo = sem("q_step"), sem("q_rot"), sem("qf_ready"), sem("q_hi"), sem("q_lo")
        k_hi, k_lo = sem("k_hi"), sem("k_lo")
        s_ready, max_ready, exp_done, rc_ready, p_norm = (sem(n) for n in (
            "s_ready", "max_ready", "exp_done", "rc_ready", "p_norm"))
        p_tr, pt_ready, o_ready, o_hi, o_lo = (sem(n) for n in ("p_tr", "pt_ready", "o_ready", "o_hi", "o_lo"))
        wo_ready, x2_ready, sq_mul, sq_sum = sem("wo_ready"), sem("x2_ready"), sem("sq_mul"), sem("sq_sum")
        sq_zero = sem("sq_zero")
        x2_hi, x2_lo = sem("x2_hi"), sem("x2_lo")
        up_ready, u_ready, tap1, tap0, conv_done, silu_done, g_ready = (sem(n) for n in (
            "up_ready", "u_ready", "tap1", "tap0", "conv_done", "silu_done", "g_ready"))
        cp_ready, u_pads = sem("cp_ready"), sem("u_pads")
        g_hi, g_lo, wd_hi, wd_lo, dn_ready, dn_free = (sem(n) for n in (
            "g_hi", "g_lo", "wd_hi", "wd_lo", "dn_ready", "dn_free"))
        x3_hi, x3_lo, x3_sq, p_tr_ready, p_hi, p_lo = (sem(n) for n in ("x3_hi", "x3_lo", "x3_sq", "p_tr_ready", "p_hi", "p_lo"))
        pl_hi, pl_lo = sem("pl_hi"), sem("pl_lo")
        gate_ready, ple_ready, gz_ready, sig_ready, gp_ready, x4_ready = (sem(n) for n in (
            "gate_ready", "ple_ready", "gz_ready", "sig_ready", "gp_ready", "x4_ready"))
        f_tr, f_sq, f_sum, f_v, f_r, f_out = (sem(n) for n in ("f_tr", "f_sq", "f_sum", "f_v", "f_r", "f_out"))

        block = ctx.enter_context(nc.Block())

        def slot(n):
            return n % 2

        def f_bank(g):
            return ps[[2, 3, 6, 7, 2, 3, 6, 7, 2, 3, 6, 7, 0, 1, 4, 5][g]]

        def mm3(pe, out, wh, wl, xh, xl, first, last):
            pe.matmul(out, wh, xh, start=first, stop=False)
            pe.matmul(out, wh, xl, start=False, stop=False)
            return pe.matmul(out, wl, xh, start=False, stop=last)

        def split_w_hi(act, n, free, count, cols=KT, base=0):
            if free is not None:
                act.wait_ge(free, count)
            act.activation(WH[:, slot(n), base:cols, :], WR[:, slot(n), base:cols, :], ACT.Copy).then_inc(w_hi, 1)

        def split_w_lo(dve, n, count, cols=KT, base=0):
            dve.wait_ge(w_hi, count + 1)
            dve.tensor_tensor(WL[:, slot(n), base:cols, :], WR[:, slot(n), base:cols, :],
                              WH[:, slot(n), base:cols, :].bitcast(F32), ALU.subtract).then_inc(w_lo, 1)

        def windows(eng, g, s, steps):
            def done(ins):
                nonlocal steps
                ins.then_inc(chain[s], 1)
                steps += 1

            eng.wait_ge(acc_free, 2 * (7 - g) + s + 1)
            u, mean_u = ub[:, s, :], PD[:, s, g, :]
            cur, lo, hi = u, 0, UB
            for k in range(g + 1):
                left, right = (1, 0) if k == 0 else (1 << (k - 1), 1 << (k - 1))
                lo, hi = lo + left, hi - right
                nxt = win[s][k % 2]
                done(eng.tensor_tensor(nxt[:, lo:hi], cur[:, lo - left:hi - left], cur[:, lo + right:hi + right], ALU.add))
                eng.wait_ge(chain[s], steps)
                cur = nxt
            e0, e1 = (col[:, CP + 2 * PAD * s + PAD * e:CP + 2 * PAD * s + PAD * (e + 1)] for e in range(2))
            done(eng.tensor_tensor(e0, cur[:, PAD:2 * PAD], edge[:, g, 0:PAD], ALU.mult))
            done(eng.tensor_tensor(e1, cur[:, S:S + PAD], edge[:, g, PAD:2 * PAD], ALU.mult))
            if s == 0:
                done(eng.scalar_tensor_tensor(mean_u, cur[:, PAD:PAD + S], 1.0 / POOL_WINDOWS[g], u[:, PAD:PAD + S],
                                              ALU.mult, ALU.subtract))
            else:
                done(eng.tensor_scalar(mean_u, cur[:, PAD:PAD + S], 1.0 / POOL_WINDOWS[g], 1.0, ALU.mult, ALU.mult))
                eng.wait_ge(chain[s], steps)
                done(eng.tensor_tensor(mean_u, mean_u, u[:, PAD:PAD + S], ALU.subtract))
            eng.wait_ge(chain[s], steps)
            eng.tensor_tensor(PD[:, s, g, 0:PAD], e0, u[:, PAD:2 * PAD], ALU.subtract)
            eng.tensor_tensor(PD[:, s, g, S - PAD:S], e1, u[:, S:S + PAD], ALU.subtract).then_inc(diff_ready[s], 1)
            eng.wait_ge(diff_ready[s], 4 - g)
            return steps

        def wtile(v):
            return v.rearrange("(k p) m -> p k m", p=P)

        @block.sync
        def _(sp):
            sp.dma_start(ident[:, :], consts["ident"]).then_inc(ident_in, 16)
            for t in range(TT):
                sp.dma_start(xtok[0][:, t, :], x[0][t * P:(t + 1) * P, :]).then_inc(x_in[t], 16)
            cols_in = [320, 256, 0, 128] + [416 + g * P for g in (3, 2, 1, 0)]
            sp.wait_ge(gains_in, 16 * 7)
            for n in range(2):
                sp.dma_start(WR[:, n, :, :], wtile(w["w_in"][:, cols_in[n]:cols_in[n] + P])).then_inc(win_in[n], 16)
            for t in range(TT):
                sp.dma_start(xtok[1][:, t, :], x[1][t * P:(t + 1) * P, :]).then_inc(x_in[TT + t], 16)
            def load_in(n):
                sp.wait_ge(w_lo, n - 1)
                sp.dma_start(WR[:, slot(n), :, :], wtile(w["w_in"][:, cols_in[n]:cols_in[n] + P])).then_inc(win_in[slot(n)], 16)

            load_in(2)
            sp.wait_ge(x_sq, 2 * TT)
            sp.dma_start(tab_q, consts["rope_q"]).then_inc(tabs_in, 16)
            sp.dma_start(tab_k, consts["rope_k"]).then_inc(tabs_in, 16)
            sp.dma_start(edge[:, :, :], consts["pool_edge"].partition_broadcast(P)).then_inc(edge_in, 16)
            sp.wait_ge(x_split, 2 * KT)
            load_in(3)
            for h in (1, 0):
                sp.dma_start(xt_dram[:, h * 4096:(h + 1) * 4096], XT[:, h * 4096:(h + 1) * 4096]).then_inc(xt_spilled[h], 16)
            for n in range(4, 8):
                load_in(n)
            sp.wait_ge(w_lo, T_POOL - 1)
            sp.dma_start(WR[:, slot(T_POOL), 4:8, :], w["pool_w"].rearrange("g c d -> c g d")).then_inc(poolw_in, 16)
            with sp.Fori(0, HEADS // 2) as i:
                sp.wait_ge(w_lo, i * 2 + (T_ATT - 1))
                for k in range(2):
                    sp.dma_start(WR[:, slot(T_ATT), 2 * k:2 * k + 2, 0:HEAD],
                                 w["w_q_b"][k * P:(k + 1) * P, bass.ds(i * 2, 2), :]).then_inc(wq_in, 16)
                sp.wait_ge(w_lo, i * 2 + T_ATT)
                sp.dma_start(WR[:, slot(T_ATT + 1), 0:2, :], w["w_kv_b"][:, bass.ds(i * 2, 2), :]).then_inc(wkv_in, 16)
            for s in range(NSEQ):
                if s == 0:
                    for n in range(T_OUT, T_OUT + 4):
                        sp.wait_ge(w_lo, n - 1)
                        sp.dma_start(WR[:, slot(n), :, :], wtile(w["w_out"][:, (n - T_OUT) * P:(n - T_OUT + 1) * P])).then_inc(ring_in[slot(n)], 16)
                    sp.wait_ge(o_lo, 2 * HEADS)
                    for q in range(4):
                        sp.dma_start(XT[:, q * 2048:(q + 1) * 2048], xt_dram[:, q * 2048:(q + 1) * 2048]).then_inc(xt_back[q], 16)
                with sp.Fori(0 if s else 2, KT // 2) as i:
                    for c in range(2):
                        n = T_OUT + s * KT + c
                        sp.wait_ge(w_lo, i * 2 + (n - 1))
                        sp.dma_start(WR[:, slot(n), :, :], wtile(w["w_out"][:, bass.ds(i * P * 2 + c * P, P)])).then_inc(ring_in[slot(n)], 16)
            def load_pair(i, first=False):
                for c in range(4):
                    n = T_UP + c
                    f = (c // 2) * P + (c % 2) * FF
                    sp.wait_ge(w_lo, i * 4 + (n - 1))
                    sp.dma_start(WR[:, slot(n), :, :], wtile(w["w_up"][:, bass.ds(i * 2 * P + f, P)])).then_inc(ring_in[slot(n)], 16)
                    if c == 1:
                        if not first:
                            sp.wait_ge(wd_lo, i)
                        sp.dma_start(WDR, w["w_down"][bass.ds(i * 2 * P, 2 * P), :].rearrange("(k p) m -> p k m", p=P)).then_inc(wd_in, 16)

            load_pair(0, first=True)
            with sp.Fori(1, NPAIR) as i:
                load_pair(i)

            def store(s):
                for t in range(TT):
                    g = s * TT + t
                    sp.wait_ge(f_out, 2 * (g + 1))
                    sp.dma_start(y[s][t * P:(t + 1) * P, :], OT[:, g % 3, :]).then_inc(out_done[g % 3], 16)

            for s in range(NSEQ):
                def gate_load(i, c):
                    n = T_GATE + s * KT + c
                    sp.wait_ge(w_lo, i * 2 + (n - 1))
                    sp.dma_start(WR[:, slot(n), :, :], wtile(w["w_ple_gate"][:, bass.ds(i * P * 2 + c * P, P)])).then_inc(ring_in[slot(n)], 16)

                def ple_load(i, c):
                    sp.dma_start(PLR[:, c], wtile(w["w_ple_proj"][:, bass.ds(i * P * 2 + c * P, P)])).then_inc(ple_in[c], 16)

                if s == 0:
                    gate_load(0, 0)
                    gate_load(0, 1)
                    sp.wait_ge(wd_lo, NPAIR)
                    ple_load(0, 0)
                    ple_load(0, 1)
                    sp.wait_ge(g_lo, 4 * NPAIR)
                else:
                    sp.wait_ge(p_tr_ready, 2)
                sp.dma_start(ptok, p_in[s].rearrange("(t p) d -> p t d", p=P)).then_inc(p_in_sem, 16)
                def both_loads(i):
                    for c in range(2):
                        gate_load(i, c)
                        sp.wait_ge(pl_lo, i * 2 + (s * KT + c - 1))
                        ple_load(i, c)

                with sp.Fori(1 - s, KT // 2 - s) as i:
                    both_loads(i)
                if s == 0:
                    sp.wait_ge(dn_ready, 16 * NPAIR)
                    sp.dma_start(gain_row, w["final_norm"].partition_broadcast(P)).then_inc(row_in, 16)
                else:
                    store(0)
                    both_loads(KT // 2 - 1)
            store(1)
            for a in range(3):
                sp.wait_ge(out_done[a], 16 * ((NSEQ * TT + 2 - a) // 3))

        @block.tensor
        def _(pe):
            def x_unit(u):
                s, f = divmod(u, KT)
                if f == 0:
                    for t in range(TT):
                        pe.wait_ge(x_in[s * TT + t], 16)
                if u >= 3:
                    pe.wait_ge(x_split, u - 2)
                b = ps[4 + u % 3]
                for t in range(TT):
                    ins = pe.transpose(b[:, t * P:(t + 1) * P], xtok[s][:, t, f * P:(f + 1) * P], ident[:, :])
                ins.then_inc(x_tr, 1)

            def in_tile(n, s, kts=range(KT), fresh=False):
                for k in kts:
                    if fresh:
                        pe.wait_ge(x_split, s * KT + k + 1)
                    ins = mm3(pe, ps[2 * (n % 2) + s][:, :], WH[:, slot(n), k, :], WL[:, slot(n), k, :],
                              XH[:, s, k, :], XL[:, s, k, :], k == 0, k == KT - 1)
                    if k == KT - 1:
                        ins.then_inc(acc_ready, 1)

            def sums(bank, s):
                for t in range(TT):
                    ins = pe.matmul(ps[bank][:, s * TT + t:s * TT + t + 1], SQ[:, s, t * P:(t + 1) * P], ones[:, 0:1],
                                    start=True, stop=True)
                return ins

            def spread(q, bank):
                pe.wait_ge(diag_ready, q + 1)
                pe.matmul(ps[bank][:, :], ones[:, :], diag[:, :, :], start=True, stop=True).then_inc(rb_ready, 1)

            pe.wait_ge(ident_in, 16)
            pe.wait_ge(gains_in, 16 * 7)
            pe.transpose(ps[7][:, 0:NPAR - N1], prow[0:NPAR - N1, 2, :], ident[0:NPAR - N1, 0:NPAR - N1]).then_inc(par_tr, 1)
            for u in range(KT):
                x_unit(u)
            pe.wait_ge(taps_in, 16 * 4)
            pe.wait_ge(par_copied, 1)
            pe.transpose(ps[7][:, 0:88], prow[0:88, 0, :], ident[0:88, 0:88])
            pe.transpose(ps[7][:, 88:176], prow[0:88, 1, :], ident[0:88, 0:88]).then_inc(par_tr, 1)
            pe.wait_ge(w_lo, 1)
            for k in range(KT):
                in_tile(0, 0, [k], fresh=True)
                x_unit(KT + k)
            in_tile(0, 1, fresh=True)
            for n in range(1, 8):
                pe.wait_ge(w_lo, n + 1)
                for s in range(NSEQ):
                    if n >= 2:
                        pe.wait_ge(acc_free, 2 * (n - 2) + s + 1)
                    in_tile(n, s)
                    if n == 1:
                        spread(B_X + s, 4 + s)
                    if s == 0 and n in (4, 6):
                        spread((B_KV if n == 4 else B_Q) + 1, 5)
                if n == 2:
                    pe.wait_ge(sq_ready, 2)
                    for s in range(NSEQ):
                        ins = sums(6, s)
                    ins.then_inc(ss_ready, 1)
                if n == 3:
                    pe.wait_ge(r_copied, 2)
                    spread(B_KV, 4)
                if n == 4:
                    pe.wait_ge(sq_ready, 4)
                    for s in range(NSEQ):
                        ins = sums(6, s)
                    ins.then_inc(ss_ready, 1)
                if n == 5:
                    pe.wait_ge(c_applied, 2)
                    spread(B_Q, 4)
            def project(i, j, first=False):
                h, s = divmod(j, 2)
                if j == 0:
                    pe.wait_ge(w_lo, i * 2 + (T_ATT + 2))
                if not first:
                    pe.wait_ge(qf_ready, i * 4 + j)
                    pe.wait_ge(k_lo, i * 4 + j)
                for k in range(2):
                    ins = mm3(pe, ps[0][:, :], WH[:, slot(T_ATT), 2 * k + h, :], WL[:, slot(T_ATT), 2 * k + h, :],
                              CHL[:, 0, k, s, :], CHL[:, 1, k, s, :], k == 0, k == 1)
                ins.then_inc(q_proj, 1)
                ins = mm3(pe, ps[1][:, :], WH[:, slot(T_ATT + 1), h, :], WL[:, slot(T_ATT + 1), h, :],
                          CHL[:, 0, 2, s, :], CHL[:, 1, 2, s, :], True, True)
                ins.then_inc(k_proj, 1)

            def values():
                for s in range(NSEQ):
                    for t in range(TT):
                        tok = slice(t * P, (t + 1) * P)
                        o = ps[4 + s][:, t * P:(t + 1) * P]
                        vh = WH[:, slot(T_ATT + 1), 0:2, NOPE:P]
                        vl = WL[:, slot(T_ATT + 1), 0:2, NOPE:P]
                        pe.matmul(o, CHL[:, 0, 2, s, tok], vh, start=True, stop=False)
                        pe.matmul(o, CHL[:, 0, 2, s, tok], vl, start=False, stop=False)
                        ins = pe.matmul(o, CHL[:, 1, 2, s, tok], vh, start=False, stop=True)
                    ins.then_inc(v_proj, 1)

            def scores(i, u, first=False):
                j, t = divmod(u, TT)
                h, s = divmod(j, 2)
                if t == 0:
                    pe.wait_ge(q_lo, i * 4 + j + 1)
                    pe.wait_ge(k_lo, i * 4 + j + 1)
                if not first:
                    pe.wait_ge(exp_done, i * 16 + u - 1)
                tok = slice(t * P, (t + 1) * P)
                ins = mm3(pe, ps[2 + u % 2][:, :], QH[0:HEAD, h, s, tok], QL[0:HEAD, h, s, tok],
                          KH[0:HEAD, h, s, :], KL[0:HEAD, h, s, :], True, True)
                ins.then_inc(s_ready, 1)

            def turn(i, u):
                pe.wait_ge(p_norm, i * 16 + u + 1)
                if u < 2:
                    pe.wait_ge(v_copied, i * 2 + u + 1)
                else:
                    pe.wait_ge(pt_ready, i * 16 + u - 1)
                for k in range(TT):
                    ins = pe.transpose(ps[4 + u % 2][:, k * P:(k + 1) * P], PB[:, u % 4, k * P:(k + 1) * P], ident[:, :])
                ins.then_inc(p_tr, 1)

            def weigh(i, j, k):
                h, s = divmod(j, 2)
                if k == 0:
                    pe.wait_ge(pt_ready, i * 16 + TT * (j + 1))
                    if j >= 2:
                        pe.wait_ge(o_lo, i * 4 + j - 1)
                    elif j == 0:
                        pe.wait_ge(v_copied, i * 2 + 2)
                ins = pe.matmul(ps[6 + j % 2][h * V_DIM:(h + 1) * V_DIM, :], VB[:, s * TT + k, h * V_DIM:(h + 1) * V_DIM],
                                PT[:, j % 2, k, :], start=(k == 0), stop=(k == TT - 1))
                if k == TT - 1:
                    ins.then_inc(o_ready, 1)

            def mix(q):
                g, s = 3 - q // 2, q % 2
                pe.wait_ge(d_lo, q + 1)
                if q >= 2:
                    pe.wait_ge(mix_lo, q - 1)
                ins = mm3(pe, ps[6 + q % 2][:, :], WH[:, slot(T_POOL), 4 + g, :], WL[:, slot(T_POOL), 4 + g, :],
                          XH[:, s, 4 + g, :], XL[:, s, 4 + g, :], True, True)
                ins.then_inc(mix_ready, 1)

            def pair(i, last):
                for u in range(4 * TT):
                    if u % TT == 2:
                        if u // TT < 2:
                            project(i, u // TT + 2)
                        elif not last:
                            project(i + 1, u // TT - 2)
                    turn(i, u)
                    if u + 3 < 4 * TT:
                        scores(i, u + 3)
                    elif not last:
                        scores(i + 1, u + 3 - 4 * TT)
                    if u >= TT:
                        weigh(i, u // TT - 1, u % TT)
                for k in range(TT):
                    weigh(i, 3, k)
                if not last:
                    values()

            pe.wait_ge(c_lo, 6)
            pe.wait_ge(kr_done, 4)
            pe.wait_ge(acc_free, 14)
            pe.wait_ge(v_ready, 3)
            project(0, 0, first=True)
            mix(0)
            mix(1)
            project(0, 1)
            mix(2)
            mix(3)
            values()
            mix(4)
            mix(5)
            pe.wait_ge(acc_free, 16)
            scores(0, 0, first=True)
            scores(0, 1, first=True)
            scores(0, 2)
            mix(6)
            mix(7)
            pe.wait_ge(mix_lo, 8)
            with pe.Fori(0, HEADS // 2 - 1) as i:
                pair(i, False)
            pair(HEADS // 2 - 1, True)

            def out_tile(s, i, c, fresh=False, first=False):
                n = T_OUT + s * KT + c
                pe.wait_ge(w_lo, i * 4 + (n + 1))
                if not fresh:
                    pe.wait_ge(x2_ready, i * 4 + (s * KT + c - 3))
                for e, k in enumerate([4, 5, 6, 7, 0, 1, 2, 3]):
                    if first and k == 0:
                        pe.wait_ge(o_lo, 4 * 3)
                    if first and k == 3:
                        pe.wait_ge(o_lo, 4 * 4)
                    ins = mm3(pe, ps[c][:, :], WH[:, slot(n), k, :], WL[:, slot(n), k, :],
                              XH[:, s, k, :], XL[:, s, k, :], e == 0, e == KT - 1)
                ins.then_inc(wo_ready, 1)

            for m in range(KT):
                out_tile(0, m // 4, m % 4, fresh=m < 4, first=m == 0)
            with pe.Fori(0, KT // 4) as i:
                for c in range(4):
                    out_tile(1, i, c)

            def up(i, c, fresh=False, seqs=range(NSEQ)):
                n = T_UP + c
                pe.wait_ge(w_lo, i * 4 + (n + 1))
                for s in seqs:
                    if c >= 2:
                        pe.wait_ge(u_ready, i * 8 + 2 * (c - 2) + s + 1)
                    elif not fresh:
                        pe.wait_ge(u_ready, i * 8 + (2 * c + s - 3))
                    for k in range(KT):
                        if fresh and c == 0:
                            pe.wait_ge(x2_lo, s * KT + k + 1)
                        ins = mm3(pe, ps[2 * (c % 2) + s][:, :], WH[:, slot(n), k, :], WL[:, slot(n), k, :],
                                  XH[:, s, k, :], XL[:, s, k, :], k == 0, k == KT - 1)
                    ins.then_inc(up_ready, 1)

            def down(i, s, last=False):
                def half(m, k):
                    ms = slice(m * P, (m + 1) * P)
                    return mm3(pe, ps[4 + (s * KT + m) % 4][:, :], WDHL[:, 0, k, ms], WDHL[:, 1, k, ms],
                               GHL[:, 0, k, s, :], GHL[:, 1, k, s, :], k == 0, k == 1)

                begun = 0
                if s == 0:
                    pe.wait_ge(wd_lo, i + 1)
                    if last:
                        pe.wait_ge(g_lo, i * 4 + 2)
                        begun = 4
                        for m in range(begun):
                            half(m, 0)
                    pe.wait_ge(g_lo, i * 4 + 4)
                for m in range(KT):
                    g = s * KT + m
                    if g >= 4:
                        pe.wait_ge(dn_free, i * 16 + g - 3)
                    if m >= begun:
                        half(m, 0)
                    half(m, 1).then_inc(dn_ready, 1)

            up(0, 0, fresh=True, seqs=[0])
            pe.wait_ge(sq_sum, 16)
            for s in range(NSEQ):
                ins = sums(6, s)
            ins.then_inc(ss_ready, 1)
            up(0, 0, fresh=True, seqs=[1])
            spread(B_X2, 4)
            up(0, 1, fresh=True, seqs=[0])
            spread(B_X2 + 1, 5)
            up(0, 1, fresh=True, seqs=[1])
            up(0, 2)
            up(0, 3)
            with pe.Fori(0, NPAIR // 2) as j:
                for i in (j * 2 + 1, j * 2 + 2):
                    up(i, 0)
                    up(i, 1)
                    down(i - 1, 0)
                    down(i - 1, 1)
                    up(i, 2)
                    up(i, 3)

            def turn_p(s):
                pe.wait_ge(p_in_sem, 16 * (s + 1))
                for k in range(2):
                    if s == 1:
                        pe.wait_ge(p_lo, k + 1)
                    for t in range(TT):
                        ins = pe.transpose(ps[2 + k][:, t * P:(t + 1) * P], ptok[:, t, k * P:(k + 1) * P], ident[:, :])
                    ins.then_inc(p_tr_ready, 1)

            down(NPAIR - 1, 0, last=True)
            pe.wait_ge(u_ready, 8 * NPAIR)
            turn_p(0)
            down(NPAIR - 1, 1)

            def gate(s, i, c):
                n = T_GATE + s * KT + c
                pe.wait_ge(w_lo, i * 2 + (n + 1))
                if not isinstance(i, int) or i > 0 or s:
                    pe.wait_ge(gz_ready, i * 2 + (s * KT + c - 1))
                for k in range(KT):
                    if s == 0 and isinstance(i, int) and i == 0 and c == 0:
                        pe.wait_ge(x3_lo, k + 1)
                    ins = mm3(pe, ps[c][:, :], WH[:, slot(n), k, :], WL[:, slot(n), k, :],
                              XH[:, s, k, :], XL[:, s, k, :], k == 0, k == KT - 1)
                ins.then_inc(gate_ready, 1)
                pe.wait_ge(pl_lo, i * 2 + (s * KT + c + 1))
                if isinstance(i, int) and i == 0 and c == 0:
                    pe.wait_ge(p_lo, 2 * s + 2)
                if not isinstance(i, int) or i > 0 or s:
                    pe.wait_ge(gp_ready, i * 2 + (s * KT + c - 1))
                for k in range(2):
                    ins = mm3(pe, ps[4 + c][:, :], PLH[:, c, k, :], PLL[:, c, k, :],
                              PH[:, k, s, :], PL[:, k, s, :], k == 0, k == 1)
                ins.then_inc(ple_ready, 1)

            def turn_x4(s, tiles=range(TT)):
                for t in tiles:
                    for h in range(2):
                        g = (s * TT + t) * 2 + h
                        if 4 <= g < 12:
                            pe.wait_ge(f_out, g - 3)
                        for f in range(4):
                            ins = pe.transpose(f_bank(g)[:, f * P:(f + 1) * P],
                                               xt[:, s, 4 * h + f, t * P:(t + 1) * P], ident[:, :])
                        ins.then_inc(f_tr, 1)

            for s in range(NSEQ):
                if s == 0:
                    pe.wait_ge(dn_free, 16 * NPAIR)
                    pe.wait_ge(sq_sum, 16 + KT)
                    sums(6, 0).then_inc(ss_ready, 1)
                else:
                    pe.wait_ge(x3_lo, 2 * KT)
                    turn_p(1)
                gate(s, 0, 0)
                if s == 0:
                    spread(B_X3, 7)
                    pe.wait_ge(v_ready, 5)
                    pe.wait_ge(sq_sum, 16 + 2 * KT)
                    sums(6, 1).then_inc(ss_ready, 1)
                gate(s, 0, 1)
                if s == 0:
                    pe.wait_ge(r_copied, 5)
                    spread(B_X3 + 1, 7)
                if s == 1:
                    pe.wait_ge(r_copied, 6)
                    pe.wait_ge(x4_ready, KT)
                    turn_x4(0, [0, 1])
                    gate(1, 1, 0)
                    gate(1, 1, 1)
                    turn_x4(0, [2, 3])
                with pe.Fori(1 + s, KT // 2) as i:
                    gate(s, i, 0)
                    gate(s, i, 1)
            pe.wait_ge(x4_ready, 2 * KT)
            turn_x4(1)

        @block.scalar
        def _(act):
            small = [("norm1", 8), ("norm2", 8), ("norm3", 8), ("q_a_norm", 2), ("kv_a_norm", 1), ("pool_scale", 4),
                     ("b_ple_gate", 8)]
            r = 0
            for name, k in small:
                act.dma_start(prow[r:r + k, 2, :], w[name].rearrange("(k p) -> k p", p=P)).then_inc(gains_in, 16)
                r += k
            taps = [w["conv_w"][k] for k in range(3)] + [w["conv_b"]]
            for k in range(4):
                h = (k % 2) * 44
                act.dma_start(prow[h:h + 44, k // 2, :], taps[k].rearrange("(k p) -> k p", p=P)).then_inc(taps_in, 16)

            def x_unit(u):
                s, f = divmod(u, KT)
                act.wait_ge(x_tr, u + 1)
                act.activation(XH[:, s, f, :], ps[4 + u % 3][:, :], ACT.Copy, scale=par[:, N1 + f:N1 + f + 1]).then_inc(x_hi, 1)

            def squares(s):
                for t in range(TT):
                    act.wait_ge(x_in[s * TT + t], 16)
                    if s + t:
                        act.wait_ge(x_sq, s * TT + t)
                    act.activation(SF[:, 4096:5120], xtok[s][:, t, :], ACT.Square,
                                   accum_out=col[:, SSX + s * TT + t:SSX + s * TT + t + 1]).then_inc(x_sq, 1)

            act.wait_ge(par_copied, 1)
            for u in range(KT):
                x_unit(u)
                if u == 3:
                    act.wait_ge(win_in[0], 16)
                    act.wait_ge(rot_done, 2)
                    split_w_hi(act, 0, None, 0)
            squares(0)
            for u in range(KT, 2 * KT):
                x_unit(u)
            act.wait_ge(win_in[1], 16)
            split_w_hi(act, 1, None, 0)
            squares(1)

            def copy_r(q, bank):
                act.wait_ge(rb_ready, q + 1)
                act.activation(R[:, q % 2, :], ps[bank][:, :], ACT.Copy).then_inc(r_copied, 1)

            copy_r(B_X, 4)
            copy_r(B_X + 1, 5)

            def c_split(c, s):
                act.activation(CHL[:, 0, c, s, :], cs[:, c, s, :], ACT.Copy).then_inc(c_hi, 1)

            for n in range(8):
                if n + 2 < 8:
                    act.wait_ge(win_in[slot(n)], 16 * ((n + 2) // 2 + 1))
                    split_w_hi(act, n + 2, acc_ready, 2 * (n + 1))
                elif n + 2 == T_POOL:
                    act.wait_ge(poolw_in, 16)
                    split_w_hi(act, T_POOL, acc_ready, 2 * (n + 1), base=4)
                if n == 0:
                    for s in range(NSEQ):
                        act.wait_ge(kr_ready, s + 1)
                        for h in range(2):
                            act.activation(KH[NOPE:HEAD, h, s, :], SQ[NOPE:HEAD, s, :], ACT.Copy).then_inc(kr_hi, 1)
                if n == 4:
                    for s in range(NSEQ):
                        act.wait_ge(c_applied, s + 1)
                        c_split(2, s)
                if n == 6:
                    for c in range(2):
                        for s in range(NSEQ):
                            act.wait_ge(c_applied, 2 + 2 * c + s + 1)
                            c_split(c, s)
            act.wait_ge(rot_done, 4)
            split_w_hi(act, T_ATT, acc_ready, 16, cols=4)
            act.wait_ge(wkv_in, 16)
            split_w_hi(act, T_ATT + 1, acc_ready, 16, cols=2)

            def k_split(i, j):
                h, s = divmod(j, 2)
                act.wait_ge(k_proj, i * 4 + j + 1)
                act.activation(KH[0:NOPE, h, s, :], ps[1][0:NOPE, :], ACT.Copy).then_inc(k_hi, 1)

            def q_split(i, j):
                h, s = divmod(j, 2)
                act.wait_ge(q_rot, i * 4 + j + 1)
                act.activation(QH[0:HEAD, h, s, :], QF[0:HEAD, j % 2, :], ACT.Copy).then_inc(q_hi, 1)

            def values(i):
                for s in range(NSEQ):
                    act.wait_ge(v_proj, i * 2 + s + 1)
                    act.activation(VB[:, s * TT:(s + 1) * TT, :], ps[4 + s][:, :].rearrange("p (k d) -> p k d", k=TT),
                                   ACT.Copy).then_inc(v_copied, 1)

            def exponent(i, u):
                act.wait_ge(max_ready, i * 16 + u + 1)
                act.activation(PB[:, u % 4, :], ps[2 + u % 2][:, :], ACT.Exp,
                               bias=col[:, NB + u % 4:NB + u % 4 + 1],
                               accum_out=col[:, RS + u % 4:RS + u % 4 + 1]).then_inc(exp_done, 1)

            def turned(i, u):
                j, t = divmod(u, TT)
                act.wait_ge(p_tr, i * 16 + u + 1)
                if t == 0 and j >= 2:
                    act.wait_ge(o_ready, i * 4 + j - 1)
                act.activation(PT[:, j % 2, :, t * P:(t + 1) * P],
                               ps[4 + u % 2][:, :].rearrange("p (k q) -> p k q", k=TT), ACT.Copy).then_inc(pt_ready, 1)

            def output(i, j):
                h, s = divmod(j, 2)
                act.wait_ge(o_ready, i * 4 + j + 1)
                act.activation(XH[h * V_DIM:(h + 1) * V_DIM, s, bass.ds(i, 1), :],
                               ps[6 + j % 2][h * V_DIM:(h + 1) * V_DIM, :], ACT.Copy).then_inc(o_hi, 1)

            def pair(i, last):
                for u in range(4 * TT):
                    if u + 2 < 4 * TT:
                        exponent(i, u + 2)
                    elif not last:
                        exponent(i + 1, u + 2 - 4 * TT)
                    turned(i, u)
                    if u % TT == 2:
                        if u // TT < 2:
                            k_split(i, u // TT + 2)
                        elif not last:
                            k_split(i + 1, u // TT - 2)
                    if u % TT == 3:
                        if u // TT < 2:
                            q_split(i, u // TT + 2)
                        elif not last:
                            q_split(i + 1, u // TT - 2)
                    if u in (8, 12):
                        output(i, (u - 8) // TT)
                    if u == 7:
                        if last:
                            act.wait_ge(ring_in[slot(T_OUT)], 16)
                        else:
                            act.wait_ge(rot_done, i * 2 + 6)
                        split_w_hi(act, T_ATT, q_proj, i * 4 + 4, cols=KT if last else 4)
                    if u == 8:
                        if last:
                            act.wait_ge(ring_in[slot(T_OUT + 1)], 16)
                        else:
                            act.wait_ge(wkv_in, i * 16 + 32)
                        split_w_hi(act, T_ATT + 1, k_proj, i * 4 + 4, cols=KT if last else 2)
                output(i, 2)
                output(i, 3)
                if not last:
                    values(i + 1)

            def diff_hi(q):
                g, s = 3 - q // 2, q % 2
                act.wait_ge(diff_ready[s], 4 - g)
                act.activation(XH[:, s, 4 + g, :], PD[:, s, g, :], ACT.Copy).then_inc(d_hi, 1)

            def mix_split(q):
                g, s = 3 - q // 2, q % 2
                act.wait_ge(mix_ready, q + 1)
                act.activation(XH[:, s, 4 + g, :], ps[6 + q % 2][:, :], ACT.Copy,
                               scale=par[:, PSC + g:PSC + g + 1]).then_inc(mix_hi, 1)

            for q in range(4):
                diff_hi(q)
            k_split(0, 0)
            q_split(0, 0)
            diff_hi(4)
            diff_hi(5)
            mix_split(0)
            mix_split(1)
            k_split(0, 1)
            q_split(0, 1)
            mix_split(2)
            mix_split(3)
            values(0)
            diff_hi(6)
            diff_hi(7)
            mix_split(4)
            mix_split(5)
            exponent(0, 0)
            exponent(0, 1)
            mix_split(6)
            mix_split(7)
            with act.Fori(0, HEADS // 2 - 1) as i:
                pair(i, False)
            pair(HEADS // 2 - 1, True)

            def ring_hi(n, more, free, count):
                act.wait_ge(ring_in[slot(n)], more * 8 + 16 * ((n - T_OUT) // 2 + 1))
                split_w_hi(act, n, free, count)

            def x_hi_of(s, m, g, done):
                act.activation(XH[:, s, bass.ds(m, 1), :], xt[:, s, bass.ds(m, 1), :], ACT.Copy,
                               scale=par[:, bass.ds(g + m, 1)]).then_inc(done, 1)

            for s in range(NSEQ):
                with act.Fori(0, KT // 4) as i:
                    for c in range(4):
                        k = s * KT + c
                        ring_hi(T_OUT + k + 2, i * 4, wo_ready, i * 4 + (k + 1))
                        if s == 1:
                            act.wait_ge(x2_ready, i * 4 + (k + 1))
                            x_hi_of(0, i * 4 + c, N2, x2_hi)
            with act.Fori(0, KT) as m:
                act.wait_ge(x2_ready, m + (KT + 1))
                x_hi_of(1, m, N2, x2_hi)
            copy_r(B_X2, 4)
            copy_r(B_X2 + 1, 5)

            def convolve(i, c):
                f, val = divmod(c, 2)
                for s in range(NSEQ):
                    t, r = i * 8 + (2 * c + s), i * 4 + (2 * f + s)
                    act.wait_ge(u_ready, t + 1)
                    if val:
                        act.wait_ge(silu_done, r + 1)
                    elif f or not isinstance(i, int):
                        act.wait_ge(g_ready, r - 1)
                    tap, bias = (col[:, CP + 2 * (2 * q + val) + f:CP + 2 * (2 * q + val) + f + 1] for q in (1, 3))
                    act.activation(C[:, s, :], U[:, s, 1:S + 1], ACT.Identity, scale=tap, bias=bias).then_inc(tap1, 1)
                for s in range(NSEQ):
                    t, r = i * 8 + (2 * c + s), i * 4 + (2 * f + s)
                    if not val:
                        act.wait_ge(conv_done, t + 1)
                        if f or not isinstance(i, int):
                            act.wait_ge(g_lo, r - 1)
                        act.activation(SG[:, s, :], C[:, s, :], ACT.Silu).then_inc(silu_done, 1)

            def g_split(i, f):
                for s in range(NSEQ):
                    act.wait_ge(g_ready, i * 4 + (2 * f + s + 1))
                    act.activation(GHL[:, 0, f, s, :], SG[:, s, :], ACT.Copy).then_inc(g_hi, 1)

            def mlp(i):
                act.wait_ge(cp_ready, i + 1)
                convolve(i, 0)
                ring_hi(T_UP + 2, i * 4, up_ready, i * 8 + 2)
                convolve(i, 1)
                ring_hi(T_UP + 3, i * 4, up_ready, i * 8 + 4)
                act.wait_ge(dn_ready, i * 16)
                g_split(i, 0)
                act.wait_ge(wd_in, i * 16 + 16)
                act.activation(WDHL[:, 0, :, :], WDR, ACT.Copy).then_inc(wd_hi, 1)
                convolve(i, 2)
                ring_hi(T_UP + 4, i * 4, up_ready, i * 8 + 6)
                convolve(i, 3)
                ring_hi(T_UP + 5, i * 4, up_ready, i * 8 + 8)
                g_split(i, 1)

            mlp(0)
            with act.Fori(1, NPAIR) as i:
                mlp(i)

            def p_split(s):
                for k in range(2):
                    act.wait_ge(p_tr_ready, 2 * s + k + 1)
                    act.activation(PH[:, k, s, :], ps[2 + k][:, :], ACT.Copy).then_inc(p_hi, 1)

            for s in range(NSEQ):
                for m in range(KT):
                    act.wait_ge(dn_free, 16 * (NPAIR - 1) + s * KT + m + 1)
                    act.activation(XH[:, s, m, :], xt[:, s, m, :], ACT.Copy,
                                   scale=par[:, N3 + m:N3 + m + 1]).then_inc(x3_hi, 1)
                    if s * KT + m >= 2:
                        act.wait_ge(sq_sum, 16 + s * KT + m - 1)
                    act.activation(sq3[m % 2], xt[:, s, m, :], ACT.Square).then_inc(x3_sq, 1)
                if s == 0:
                    p_split(0)

            def ple_hi(i, c, free, count):
                act.wait_ge(ple_in[c], i * 16 + 16)
                act.wait_ge(free, count)
                act.activation(PLH[:, c], PLR[:, c], ACT.Copy).then_inc(pl_hi, 1)

            def gate(s, i, c, more=True):
                k = s * KT + c
                if more:
                    ring_hi(T_GATE + k + 2, i * 2, gate_ready, i * 2 + (k + 1))
                act.wait_ge(gz_ready, i * 2 + (k + 1))
                if s or not isinstance(i, int):
                    act.wait_ge(x4_ready, i * 2 + (k - 1))
                act.activation(GS[c], GZ[:, c, :], ACT.Sigmoid, bias=par[:, bass.ds(i * 2 + (BG + c), 1)]).then_inc(sig_ready, 1)
                if more:
                    ple_hi(i + (s * KT // 2 + 1), c, ple_ready, i * 2 + (k + 1))

            def finish(tiles):
                for t in tiles:
                    for h in range(2):
                        g = 2 * t + h
                        act.wait_ge(f_tr, g + 1)
                        if g >= 2:
                            act.wait_ge(f_sq, g - 1)
                        act.activation(SQ[:, h, :], f_bank(g)[:, :], ACT.Square,
                                       accum_out=col[:, FS + g:FS + g + 1]).then_inc(f_sq, 1)

            for c in range(2):
                ple_hi(0, c, dn_ready, 16 * NPAIR)
            for s in range(NSEQ):
                if s == 1:
                    p_split(1)
                if s == 0:
                    copy_r(B_X3, 7)
                gate(s, 0, 0)
                gate(s, 0, 1)
                if s == 0:
                    copy_r(B_X3 + 1, 7)
                if s == 1:
                    finish([0, 1])
                    gate(1, 1, 0)
                    gate(1, 1, 1)
                    finish([2, 3])
                with act.Fori(1 + s, KT // 2 - s) as i:
                    gate(s, i, 0)
                    gate(s, i, 1)
            for c in range(2):
                gate(1, KT // 2 - 1, c, more=False)
            finish(range(TT, 2 * TT))

        @block.vector
        def _(dve):
            def f32(v):
                return v.bitcast(F32)

            dve.memset(ones[:, :], 1.0).then_inc(consts_set, 1)
            dve.memset(col[:, HALF:HALF + 8], -0.5).then_inc(consts_set, 1)
            dve.wait_ge(par_tr, 1)
            dve.tensor_copy(par[:, N1:NPAR], ps[7][:, 0:NPAR - N1]).then_inc(par_copied, 1)
            dve.wait_ge(par_copied, 1)

            def x_unit(u):
                s, f = divmod(u, KT)
                dve.wait_ge(x_hi, u + 1)
                dve.tensor_copy(xt[:, s, f, :], ps[4 + u % 3][:, :])
                dve.scalar_tensor_tensor(XL[:, s, f, :], ps[4 + u % 3][:, :], par[:, N1 + f:N1 + f + 1],
                                         f32(XH[:, s, f, :]), ALU.mult, ALU.subtract).then_inc(x_split, 1)

            for u in range(KT):
                x_unit(u)
                if u == 4:
                    split_w_lo(dve, 0, 0)
            dve.wait_ge(par_tr, 2)
            dve.tensor_copy(par[:, 0:N1], ps[7][:, 0:N1]).then_inc(par_copied, 1)
            for u in range(KT, 2 * KT):
                x_unit(u)
            split_w_lo(dve, 1, 1)

            def mean(out, total, n, done=None):
                dve.tensor_scalar(out, total, 1.0 / n, EPS, ALU.mult, ALU.add).then_inc(done, 1)

            def diagonal(q, cols):
                dve.wait_ge(col_ready, cols)
                if q:
                    dve.wait_ge(rb_ready, q)
                for t in range(TT):
                    ins = dve.tensor_scalar(diag[:, t, :], ident[:, :], col[:, R_COL + 4 * q + t:R_COL + 4 * q + t + 1], None, ALU.mult)
                ins.then_inc(diag_ready, 1)

            dve.wait_ge(x_sq, 2 * TT)
            mean(col[:, V_COL:V_COL + 8], col[:, SSX:SSX + 8], D, v_ready)
            diagonal(B_X, 1)
            diagonal(B_X + 1, 1)
            for s in range(NSEQ):
                dve.memset(ub[:, s, 0:PAD], 0.0)
                ins = dve.memset(ub[:, s, PAD + S:UB], 0.0)
            ins.then_inc(pads_zero, 1)
            dve.wait_ge(tabs_in, 32)

            def times_r(n, s, out):
                dve.wait_ge(r_copied, s + 1)
                dve.wait_ge(acc_ready, 2 * n + s + 1)
                return dve.tensor_tensor(out, ps[2 * (n % 2) + s][:, :], R[:, s, :], ALU.mult).then_inc(acc_free, 1)

            chained = 0
            for n in range(8):
                if n == 0:
                    split_w_lo(dve, 2, 2)
                    for s in range(NSEQ):
                        kr = (w1, w2)[s][:, 0:S]
                        times_r(n, s, kr)
                        dve.wait_ge(acc_free, s + 1)
                        if s:
                            dve.wait_ge(kr_ready, s)
                        dve.tensor_tensor(SQT[NOPE:HEAD, :], kr[HEAD:P, :], tab_k[HEAD:P, :], ALU.mult).then_inc(kr_step, 1)
                        dve.tensor_tensor(SQ[NOPE:HEAD, s, :], kr[NOPE:HEAD, :], tab_k[NOPE:HEAD, :], ALU.mult).then_inc(kr_step, 1)
                        dve.wait_ge(kr_step, 2 * s + 2)
                        dve.tensor_tensor(SQ[NOPE:HEAD, s, :], SQ[NOPE:HEAD, s, :], SQT[NOPE:HEAD, :], ALU.add).then_inc(kr_ready, 1)
                    for s in range(NSEQ):
                        for h in range(2):
                            dve.wait_ge(kr_hi, 2 * s + h + 1)
                            dve.tensor_tensor(KL[NOPE:HEAD, h, s, :], SQ[NOPE:HEAD, s, :], f32(KH[NOPE:HEAD, h, s, :]),
                                              ALU.subtract).then_inc(kr_done, 1)
                elif n < 4:
                    c = (2, 0, 1)[n - 1]
                    if n == 1:
                        dve.wait_ge(xt_spilled[1], 16)
                    for s in range(NSEQ):
                        times_r(n, s, cs[:, c, s, :])
                        dve.wait_ge(acc_free, 2 * n + s + 1)
                else:
                    if n == 4:
                        dve.wait_ge(xt_spilled[0], 16)
                        dve.wait_ge(pads_zero, 1)
                        dve.wait_ge(edge_in, 16)
                    if n == 7:
                        split_w_lo(dve, T_ATT, T_ATT, cols=4)
                        split_w_lo(dve, T_ATT + 1, T_ATT + 1, cols=2)
                        chained = windows(dve, 1, 0, chained)
                    for s in range(NSEQ):
                        if n > 4:
                            dve.wait_ge(diff_ready[s], n - 4)
                        times_r(n, s, ub[:, s, PAD:PAD + S])
                if 0 < n <= T_POOL - 2:
                    split_w_lo(dve, n + 2, n + 2, base=0 if n + 2 < T_POOL else 4)
                if n == 2:
                    dve.wait_ge(ss_ready, 1)
                    mean(col[:, V_COL + 8:V_COL + 16], ps[6][:, 0:8], KV_RANK, v_ready)
                    diagonal(B_KV, 2)
                if n == 3:
                    diagonal(B_KV + 1, 2)
                if n == 4:
                    for s in range(NSEQ):
                        dve.wait_ge(rb_ready, B_KV + s + 1)
                        dve.scalar_tensor_tensor(cs[:, 2, s, :], cs[:, 2, s, :], par[:, GKV:GKV + 1], ps[4 + s][:, :],
                                                 ALU.mult, ALU.mult).then_inc(c_applied, 1)
                    for s in range(NSEQ):
                        dve.wait_ge(c_hi, s + 1)
                        dve.tensor_tensor(CHL[:, 1, 2, s, :], cs[:, 2, s, :], f32(CHL[:, 0, 2, s, :]), ALU.subtract).then_inc(c_lo, 1)
                    dve.wait_ge(ss_ready, 2)
                    mean(col[:, V_COL + 16:V_COL + 24], ps[6][:, 0:8], Q_RANK, v_ready)
                if n == 5:
                    diagonal(B_Q + 1, 3)
                if n == 6:
                    dve.wait_ge(rb_ready, B_Q + 2)
                    for c in range(2):
                        for s in range(NSEQ):
                            dve.scalar_tensor_tensor(cs[:, c, s, :], cs[:, c, s, :], par[:, GQ + c:GQ + c + 1], ps[4 + s][:, :],
                                                     ALU.mult, ALU.mult).then_inc(c_applied, 1)
                    for c in range(2):
                        for s in range(NSEQ):
                            dve.wait_ge(c_hi, 2 + 2 * c + s + 1)
                            dve.tensor_tensor(CHL[:, 1, c, s, :], cs[:, c, s, :], f32(CHL[:, 0, c, s, :]),
                                              ALU.subtract).then_inc(c_lo, 1)
                if n in (4, 5):
                    chained = windows(dve, 7 - n, 0, chained)
                if n == 4:
                    diagonal(B_Q, 3)
            def rotate(i, j):
                dve.wait_ge(q_proj, i * 4 + j + 1)
                if not isinstance(i, int) or i or j:
                    dve.wait_ge(q_rot, i * 4 + j)
                dve.tensor_tensor(QF[0:HEAD, j % 2, :], ps[0][0:HEAD, :], tab_q[0:HEAD, :], ALU.mult).then_inc(q_step, 1)
                dve.tensor_tensor(QTMP[NOPE:HEAD, :], ps[0][HEAD:P, :], tab_q[HEAD:P, :], ALU.mult).then_inc(qf_ready, 1)
                dve.wait_ge(q_step, i * 4 + j + 1)
                dve.wait_ge(qf_ready, i * 4 + j + 1)
                dve.tensor_tensor(QF[NOPE:HEAD, j % 2, :], QF[NOPE:HEAD, j % 2, :], QTMP[NOPE:HEAD, :],
                                  ALU.add).then_inc(q_rot, 1)

            def lows(i, j):
                h, s = divmod(j, 2)
                dve.wait_ge(k_hi, i * 4 + j + 1)
                dve.tensor_tensor(KL[0:NOPE, h, s, :], ps[1][0:NOPE, :], f32(KH[0:NOPE, h, s, :]), ALU.subtract).then_inc(k_lo, 1)
                dve.wait_ge(q_hi, i * 4 + j + 1)
                dve.tensor_tensor(QL[0:HEAD, h, s, :], QF[0:HEAD, j % 2, :], f32(QH[0:HEAD, h, s, :]),
                                  ALU.subtract).then_inc(q_lo, 1)

            def maximum(i, u):
                dve.wait_ge(s_ready, i * 16 + u + 1)
                dve.tensor_reduce(col[:, NB + u % 4:NB + u % 4 + 1], ps[2 + u % 2][:, :], AX_X, ALU.max,
                                  negate=True).then_inc(max_ready, 1)

            def normalise(i, u):
                dve.wait_ge(exp_done, i * 16 + u + 1)
                dve.reciprocal(col[:, RC + u % 4:RC + u % 4 + 1], col[:, RS + u % 4:RS + u % 4 + 1]).then_inc(rc_ready, 1)
                dve.wait_ge(rc_ready, i * 16 + u + 1)
                dve.tensor_scalar(PB[:, u % 4, :], PB[:, u % 4, :], col[:, RC + u % 4:RC + u % 4 + 1], None,
                                  ALU.mult).then_inc(p_norm, 1)

            def output(i, j):
                h, s = divmod(j, 2)
                rows = slice(h * V_DIM, (h + 1) * V_DIM)
                dve.wait_ge(o_hi, i * 4 + j + 1)
                dve.tensor_tensor(XL[rows, s, bass.ds(i, 1), :], ps[6 + j % 2][rows, :],
                                  f32(XH[rows, s, bass.ds(i, 1), :]), ALU.subtract).then_inc(o_lo, 1)

            def pair(i, last):
                for u in range(4 * TT):
                    normalise(i, u)
                    if u + 2 < 4 * TT:
                        maximum(i, u + 2)
                    elif not last:
                        maximum(i + 1, u + 2 - 4 * TT)
                    if u % TT == 0:
                        if u // TT < 3:
                            lows(i, u // TT + 1)
                        elif not last:
                            lows(i + 1, 0)
                    if u % TT == 2:
                        if u // TT < 2:
                            rotate(i, u // TT + 2)
                        elif not last:
                            rotate(i + 1, u // TT - 2)
                    if u in (9, 13):
                        output(i, (u - 8) // TT)
                    if u == 9:
                        split_w_lo(dve, T_ATT, i * 2 + (T_ATT + 2), cols=KT if last else 4)
                    if u == 9:
                        split_w_lo(dve, T_ATT + 1, i * 2 + (T_ATT + 3), cols=KT if last else 2)
                output(i, 2)
                output(i, 3)

            def mix_low(q):
                g, s = 3 - q // 2, q % 2
                dve.wait_ge(mix_hi, q + 1)
                dve.scalar_tensor_tensor(XL[:, s, 4 + g, :], ps[6 + q % 2][:, :], par[:, PSC + g:PSC + g + 1],
                                         f32(XH[:, s, 4 + g, :]), ALU.mult, ALU.subtract).then_inc(mix_lo, 1)

            rotate(0, 0)
            lows(0, 0)
            mix_low(0)
            mix_low(1)
            rotate(0, 1)
            windows(dve, 0, 0, chained)
            for q in range(2, 6):
                mix_low(q)
            maximum(0, 0)
            maximum(0, 1)
            mix_low(6)
            mix_low(7)
            with dve.Fori(0, HEADS // 2 - 1) as i:
                pair(i, False)
            pair(HEADS // 2 - 1, True)

            def x_lo_of(s, m, g, hi, count, done):
                dve.wait_ge(hi, count)
                dve.scalar_tensor_tensor(XL[:, s, bass.ds(m, 1), :], xt[:, s, bass.ds(m, 1), :], par[:, bass.ds(g + m, 1)],
                                         f32(XH[:, s, bass.ds(m, 1), :]), ALU.mult, ALU.subtract).then_inc(done, 1)

            for s in range(NSEQ):
                for h in range(2):
                    dve.wait_ge(xt_back[2 * s + h], 16)
                with dve.Fori(0, KT // 4) as i:
                    for c in range(4):
                        k = s * KT + c
                        dve.wait_ge(wo_ready, i * 4 + (k + 1))
                        dve.tensor_tensor(xt[:, s, bass.ds(i * 4 + c, 1), :], xt[:, s, bass.ds(i * 4 + c, 1), :], ps[c][:, :],
                                          ALU.add).then_inc(x2_ready, 1)
                        split_w_lo(dve, T_OUT + k + 2, i * 4 + (T_OUT + k + 2))
                        if s == 1:
                            x_lo_of(0, i * 4 + c, N2, x2_hi, i * 4 + (c + 1), x2_lo)
            with dve.Fori(0, KT) as m:
                x_lo_of(1, m, N2, x2_hi, m + (KT + 1), x2_lo)

            dve.wait_ge(ss_ready, 3)
            mean(col[:, V_COL + 24:V_COL + 32], ps[6][:, 0:8], D, v_ready)
            diagonal(B_X2, 4)
            for s in range(NSEQ):
                dve.memset(U[:, s, 0:1], 0.0)
                ins = dve.memset(U[:, s, S + 1:S + 2], 0.0)
            ins.then_inc(u_pads, 1)
            diagonal(B_X2 + 1, 4)

            def scaled(i, c, s):
                t = i * 8 + (2 * c + s)
                dve.wait_ge(up_ready, t + 1)
                if c or not isinstance(i, int):
                    dve.wait_ge(conv_done, t - 1)
                dve.tensor_tensor(U[:, s, 1:S + 1], ps[2 * (c % 2) + s][:, :], R[:, s, :], ALU.mult).then_inc(u_ready, 1)

            def taps(i, c):
                f, val = divmod(c, 2)
                tap_l, tap_r = (col[:, CP + 2 * (2 * q + val) + f:CP + 2 * (2 * q + val) + f + 1] for q in (0, 2))
                for s in range(NSEQ):
                    t = i * 8 + (2 * c + s)
                    dve.wait_ge(tap1, t + 1)
                    dve.scalar_tensor_tensor(C[:, s, :], U[:, s, 0:S], tap_l, C[:, s, :], ALU.mult, ALU.add).then_inc(tap0, 1)
                for s in range(NSEQ):
                    t = i * 8 + (2 * c + s)
                    dve.wait_ge(tap0, t + 1)
                    dve.scalar_tensor_tensor(C[:, s, :], U[:, s, 2:S + 2], tap_r, C[:, s, :], ALU.mult, ALU.add).then_inc(conv_done, 1)

            def product(i, f):
                for s in range(NSEQ):
                    r = i * 4 + (2 * f + s)
                    dve.wait_ge(silu_done, r + 1)
                    dve.wait_ge(conv_done, i * 8 + (2 * (2 * f + 1) + s + 1))
                    dve.tensor_tensor(SG[:, s, :], SG[:, s, :], C[:, s, :], ALU.mult).then_inc(g_ready, 1)

            def g_lows(i, f):
                for s in range(NSEQ):
                    dve.wait_ge(g_hi, i * 4 + (2 * f + s + 1))
                    dve.tensor_tensor(GHL[:, 1, f, s, :], SG[:, s, :], f32(GHL[:, 0, f, s, :]), ALU.subtract).then_inc(g_lo, 1)

            def add_down(i, s, m):
                g = s * KT + m
                dve.wait_ge(dn_ready, i * 16 + (g + 1))
                dve.tensor_tensor(xt[:, s, m, :], xt[:, s, m, :], ps[4 + g % 4][:, :], ALU.add).then_inc(dn_free, 1)

            def mlp(i, first):
                for c in range(4):
                    f, val = divmod(c, 2)
                    for s in range(NSEQ):
                        if first and c == 0:
                            dve.wait_ge(r_copied, s + 3)
                        scaled(i, c, s)
                    taps(i, c)
                    if c == 1 and not first:
                        add_down(i - 1, 0, 0)
                        add_down(i - 1, 0, 1)
                    if val:
                        product(i, f)
                    split_w_lo(dve, T_UP + c + 2, i * 4 + (T_UP + c + 2))
                    if c == 1:
                        if not first:
                            for g in range(2, NSEQ * KT):
                                add_down(i - 1, g // KT, g % KT)
                        g_lows(i, 0)
                        dve.wait_ge(wd_hi, i + 1)
                        dve.tensor_tensor(WDHL[:, 1, :, :], WDR, f32(WDHL[:, 0, :, :]), ALU.subtract).then_inc(wd_lo, 1)
                    if c == 3:
                        g_lows(i, 1)

            dve.wait_ge(u_pads, 1)
            mlp(0, True)
            with dve.Fori(1, NPAIR) as i:
                mlp(i, False)

            def p_lows(s):
                for k in range(2):
                    dve.wait_ge(p_hi, 2 * s + k + 1)
                    dve.tensor_tensor(PL[:, k, s, :], ps[2 + k][:, :], f32(PH[:, k, s, :]), ALU.subtract).then_inc(p_lo, 1)

            def x3_low(k):
                s, m = divmod(k, KT)
                dve.wait_ge(x3_hi, k + 1)
                dve.scalar_tensor_tensor(XL[:, s, m, :], xt[:, s, m, :], par[:, N3 + m:N3 + m + 1], f32(XH[:, s, m, :]),
                                         ALU.mult, ALU.subtract).then_inc(x3_lo, 1)

            for k in range(2 * KT):
                add_down(NPAIR - 1, k // KT, k % KT)
                if k:
                    x3_low(k - 1)
                if k == KT:
                    p_lows(0)
            x3_low(2 * KT - 1)

            def ple_low(i, c):
                dve.wait_ge(pl_hi, i * 2 + (c + 1))
                dve.tensor_tensor(PLL[:, c], PLR[:, c], f32(PLH[:, c]), ALU.subtract).then_inc(pl_lo, 1)

            def gate(s, i, c, more=True):
                k = s * KT + c
                m = i * 2 + c
                dve.wait_ge(gate_ready, i * 2 + (k + 1))
                if s or not isinstance(i, int):
                    dve.wait_ge(sig_ready, i * 2 + (k - 1))
                dve.tensor_tensor(GZ[:, c, :], ps[c][:, :], R[:, s, :], ALU.mult).then_inc(gz_ready, 1)
                if more:
                    split_w_lo(dve, T_GATE + k + 2, i * 2 + (T_GATE + k + 2))
                dve.wait_ge(ple_ready, i * 2 + (k + 1))
                dve.wait_ge(sig_ready, i * 2 + (k + 1))
                dve.tensor_tensor(GS[c], ps[4 + c][:, :], GS[c], ALU.mult).then_inc(gp_ready, 1)
                dve.wait_ge(gp_ready, i * 2 + (k + 1))
                dve.tensor_tensor(xt[:, s, bass.ds(m, 1), :], xt[:, s, bass.ds(m, 1), :], GS[c], ALU.add).then_inc(x4_ready, 1)
                if more:
                    ple_low(i + (s * KT // 2 + 1), c)

            def finish(tiles):
                def stats(t):
                    dve.wait_ge(f_sq, 2 * t + 2)
                    dve.tensor_tensor(col[:, FV + t:FV + t + 1], col[:, FS + 2 * t:FS + 2 * t + 1],
                                      col[:, FS + 2 * t + 1:FS + 2 * t + 2], ALU.add).then_inc(f_sum, 1)
                    dve.wait_ge(f_sum, t + 1)
                    mean(col[:, FV + t:FV + t + 1], col[:, FV + t:FV + t + 1], D, f_v)

                stats(tiles[0])
                for t in tiles:
                    if t + 1 in tiles:
                        stats(t + 1)
                    dve.wait_ge(f_r, t + 1)
                    if t >= 3:
                        dve.wait_ge(out_done[t % 3], 16 * (t // 3))
                    for h in range(2):
                        cols = slice(h * S, (h + 1) * S)
                        dve.scalar_tensor_tensor(OT[:, t % 3, cols], f_bank(2 * t + h)[:, :],
                                                 col[:, FR + t:FR + t + 1], gain_row[:, cols], ALU.mult, ALU.mult).then_inc(f_out, 1)

            def norm3(s):
                dve.wait_ge(ss_ready, 4 + s)
                mean(col[:, V_COL + 32 + 4 * s:V_COL + 36 + 4 * s], ps[6][:, 4 * s:4 * s + 4], D, v_ready)
                diagonal(B_X3 + s, 5 + s)

            for c in range(2):
                ple_low(0, c)
            for s in range(NSEQ):
                if s == 1:
                    p_lows(1)
                if s == 0:
                    norm3(0)
                dve.wait_ge(r_copied, 5 + s)
                gate(s, 0, 0)
                if s == 0:
                    norm3(1)
                gate(s, 0, 1)
                if s == 1:
                    dve.wait_ge(row_in, 16)
                    finish([0, 1])
                    gate(1, 1, 0)
                    gate(1, 1, 1)
                    finish([2, 3])
                with dve.Fori(1 + s, KT // 2 - s) as i:
                    gate(s, i, 0)
                    gate(s, i, 1)
            for c in range(2):
                gate(1, KT // 2 - 1, c, more=False)
            finish(range(TT, 2 * TT))

        @block.gpsimd
        def _(pool):
            def rot_columns(n, k):
                q = ROPE // 2
                pool.tensor_scalar(WR[:, slot(n), 0:k, HEAD:HEAD + q], WR[:, slot(n), 0:k, HEAD - q:HEAD], -1.0, 1.0,
                                   ALU.mult, ALU.mult).then_inc(rot_done, 1)
                pool.tensor_copy(WR[:, slot(n), 0:k, HEAD + q:P], WR[:, slot(n), 0:k, NOPE:NOPE + q]).then_inc(rot_done, 1)

            def root(q, n, count):
                pool.wait_ge(v_ready, count)
                pool.tensor_tensor(col[:, R_COL + 4 * q:R_COL + 4 * q + n], col[:, V_COL + 4 * q:V_COL + 4 * q + n],
                                   col[:, HALF:HALF + n], ALU.pow).then_inc(col_ready, 1)

            pool.wait_ge(win_in[0], 16)
            rot_columns(T_IN, KT)
            pool.wait_ge(consts_set, 2)
            root(B_X, 8, 1)
            pool.wait_ge(kr_done, 4)
            for s in range(NSEQ):
                pool.wait_ge(acc_free, 2 + s + 1)
                pool.tensor_tensor(SQ[:, s, :], cs[:, 2, s, :], cs[:, 2, s, :], ALU.mult).then_inc(sq_ready, 1)
            root(B_KV, 8, 2)
            for s in range(NSEQ):
                pool.wait_ge(acc_free, 6 + s + 1)
                pool.tensor_tensor(SQ[:, s, :], cs[:, 0, s, :], cs[:, 0, s, :], ALU.mult).then_inc(sq_part, 1)
                if s:
                    pool.wait_ge(sq_ready, 3)
                pool.tensor_tensor(SQT, cs[:, 1, s, :], cs[:, 1, s, :], ALU.mult).then_inc(sq_part, 1)
                pool.wait_ge(sq_part, 2 * s + 2)
                pool.tensor_tensor(SQ[:, s, :], SQ[:, s, :], SQT, ALU.add).then_inc(sq_ready, 1)
            root(B_Q, 8, 3)
            pool.wait_ge(xt_spilled[0], 16)
            pool.wait_ge(pads_zero, 1)
            pool.wait_ge(edge_in, 16)
            chained = 0
            for g in (3, 2, 1):
                chained = windows(pool, g, 1, chained)
            pool.wait_ge(wq_in, 32)
            rot_columns(T_ATT, 4)

            def diff_low(q):
                g, s = 3 - q // 2, q % 2
                pool.wait_ge(d_hi, q + 1)
                pool.tensor_tensor(XL[:, s, 4 + g, :], PD[:, s, g, :], XH[:, s, 4 + g, :].bitcast(F32), ALU.subtract).then_inc(d_lo, 1)

            for q in range(4):
                diff_low(q)
            windows(pool, 0, 1, chained)
            for q in range(4, 8):
                diff_low(q)

            for i in range(1, HEADS // 2):
                pool.wait_ge(wq_in, i * 32 + 32)
                rot_columns(T_ATT, 4)

            def squares(s, m, ready, count, done):
                pool.wait_ge(ready, count)
                pool.tensor_tensor(SQT, xt[:, s, bass.ds(m, 1), :], xt[:, s, bass.ds(m, 1), :], ALU.mult).then_inc(sq_mul, 1)
                pool.wait_ge(sq_mul, done)
                pool.tensor_tensor(SQ[:, s, :], SQ[:, s, :], SQT, ALU.add).then_inc(sq_sum, 1)
                pool.wait_ge(sq_sum, done)

            pool.memset(SQ[:, :, :], 0.0).then_inc(sq_zero, 1)
            pool.wait_ge(sq_zero, 1)
            for s in range(NSEQ):
                with pool.Fori(0, KT) as m:
                    squares(s, m, x2_ready, m + (s * KT + 1), m + (s * KT + 1))
            root(B_X2, 8, 4)

            def place_taps(i, first=False):
                if not first:
                    pool.wait_ge(conv_done, i * 8)
                pool.tensor_copy(col[:, CP:CP + 16].rearrange("p (k f) -> p k f", f=2),
                                 par[:, 0:N1].rearrange("p (k f) -> p k f", f=FT)[:, :, bass.ds(i * 2, 2)]).then_inc(cp_ready, 1)

            place_taps(0, first=True)
            with pool.Fori(1, NPAIR) as i:
                place_taps(i)

            pool.wait_ge(g_ready, 4 * NPAIR)
            pool.memset(SQ[:, :, :], 0.0).then_inc(sq_zero, 1)
            pool.wait_ge(sq_zero, 2)
            for k in range(NSEQ * KT):
                s = k // KT
                pool.wait_ge(x3_sq, k + 1)
                pool.tensor_tensor(SQ[:, s, :], SQ[:, s, :], sq3[k % 2], ALU.add).then_inc(sq_sum, 1)
                pool.wait_ge(sq_sum, 16 + k + 1)
            root(B_X3, 4, 5)
            root(B_X3 + 1, 4, 6)
            for t in range(NSEQ * TT):
                pool.wait_ge(f_v, t + 1)
                pool.tensor_tensor(col[:, FR + t:FR + t + 1], col[:, FV + t:FV + t + 1], col[:, HALF:HALF + 1],
                                   ALU.pow).then_inc(f_r, 1)


_WEIGHTS = ["norm1", "w_in", "q_a_norm", "w_q_b", "kv_a_norm", "w_kv_b", "pool_w", "pool_scale", "w_out", "norm2",
            "w_up", "conv_w", "conv_b", "w_down", "norm3", "w_ple_gate", "b_ple_gate", "w_ple_proj", "final_norm"]


def _constants():
    inv = 1.0 / (10000.0 ** (np.arange(0, ROPE, 2, dtype=np.float32) / ROPE))
    ang = np.arange(S, dtype=np.float32)[:, None] * inv[None, :]
    emb = np.concatenate([ang, ang], axis=-1).T
    cos, sin = np.cos(emb).astype(np.float32), np.sin(emb).astype(np.float32)
    scale = np.float32(HEAD ** -0.5)
    rope_k = np.concatenate([np.ones((NOPE, S), np.float32), cos, sin])
    edge = np.zeros((4, 2 * PAD), np.float32)
    t = np.concatenate([np.arange(PAD), np.arange(S - PAD, S)])
    for g, w in enumerate(POOL_WINDOWS):
        edge[g] = 1.0 / (np.clip(t - w // 2 + w, 0, S) - np.clip(t - w // 2, 0, S)).astype(np.float32)
    return {"ident": np.eye(P, dtype=np.float32), "rope_k": rope_k, "rope_q": rope_k * scale, "pool_edge": edge}


def kernel(**inputs):
    import concourse.bacc as _bacc
    from concourse.bass_utils import run_bass_kernel_spmd as _run

    nc = _bacc.Bacc("TRN2", target_bir_lowering=False, num_devices=1)
    arrays = {}

    def dram(name, a):
        a = np.ascontiguousarray(a)
        arrays[f"in_{name}"] = a
        return nc.dram_tensor(f"in_{name}", a.shape, mybir.dt.from_np(a.dtype), kind="ExternalInput").ap()

    x = [dram(n, np.asarray(inputs[n])[0]) for n in ("x_prompt", "x_sample")]
    p_in = [dram(n, np.asarray(inputs[n])[0, 0]) for n in ("p_prompt", "p_sample")]
    w = {n: dram(n, np.asarray(inputs[n])[0] if n != "final_norm" else np.asarray(inputs[n])) for n in _WEIGHTS}
    consts = {n: dram(n, a) for n, a in _constants().items()}
    y = [nc.dram_tensor(f"out_{i}", (S, D), F32, kind="ExternalOutput").ap() for i in range(NSEQ)]
    encoder(nc, x, p_in, w, y, consts)
    r = _run(nc, [arrays], core_ids=[0])
    return tuple(r.results[0][f"out_{i}"].reshape(1, S, D) for i in range(NSEQ))
```
